# Optimizing a Trainium2 kernel written in Bass

```python
import jax, jax.numpy as jnp
from jax import lax
import numpy as np

D_MODEL = 1024
BATCH = 1
SEQ = 128
DEPTH = 2
DEC_BATCH = 1
DEC_SEQ = 512
PAST_LEN = 128

GRID_W = 64
CONV_WIDTH = 256
NA_HEADS = 4
NA_HEAD_DIM = 64
NA_WIDTH = NA_HEADS * NA_HEAD_DIM
NA_KH = 8
NA_KW = 16
MLA_HEADS = 4
MLA_Q_LORA = 256
MLA_KV_LORA = 128
MLA_NOPE_DIM = 64
MLA_ROPE_DIM = 32
MLA_V_DIM = 64
MLA_WIDTH = MLA_HEADS * MLA_V_DIM
FN_GROUPS = 4
FN_GROUP_DIM = 64
FN_WIDTH = FN_GROUPS * FN_GROUP_DIM
MIX_WIDTH = CONV_WIDTH + NA_WIDTH + MLA_WIDTH + FN_WIDTH
PROJ_SIZES = (CONV_WIDTH, CONV_WIDTH, CONV_WIDTH, NA_WIDTH, NA_WIDTH, NA_WIDTH, MLA_Q_LORA, MLA_KV_LORA, MLA_ROPE_DIM, FN_WIDTH)
PROJ_WIDTH = sum(PROJ_SIZES)
N_EXPERTS = 16
N_EXPERT_GROUPS = 4
EXPERTS_PER_GROUP = N_EXPERTS // N_EXPERT_GROUPS
TOP_K = 2
EXPERT_FF = 256
ROPE_THETA = 10000.0
Q_BLOCK = 128
EPS = 1e-6
NEG_INF = -1e30

kernel_name = 'hybrid_flow_conv_na_mla_fnet_moe_step'

def rmsnorm(x, g):
    xf = x.astype(jnp.float32)
    y = xf * lax.rsqrt(jnp.mean(xf * xf, axis=-1, keepdims=True) + EPS)
    return (y * g.astype(jnp.float32)).astype(x.dtype)

def ada_modulation(cond, w_ada, b_ada):
    m = jax.nn.silu(cond) @ w_ada + b_ada
    return [t[:, None, :] for t in jnp.split(m, 6, axis=-1)]

def modulate(x, g, shift, scale):
    return rmsnorm(x, g) * (1 + scale) + shift

def split_projection(p):
    idx, acc = [], 0
    for s in PROJ_SIZES[:-1]:
        acc += s
        idx.append(acc)
    return jnp.split(p, idx, axis=-1)

def axial_rope_tables(n):
    t = jnp.arange(n)
    pos = jnp.stack([t // GRID_W, t % GRID_W], axis=-1).astype(jnp.float32)
    nf = MLA_ROPE_DIM // 4
    freqs = ROPE_THETA ** (-jnp.arange(nf, dtype=jnp.float32) / nf)
    ang = pos[:, :, None] * freqs
    return jnp.cos(ang), jnp.sin(ang)

def apply_axial_rope(x, cos, sin):
    shp = x.shape
    xr = x.astype(jnp.float32).reshape(shp[:-1] + (2, 2, MLA_ROPE_DIM // 4))
    x1, x2 = xr[..., 0, :], xr[..., 1, :]
    out = jnp.stack([x1 * cos - x2 * sin, x2 * cos + x1 * sin], axis=-2)
    return out.reshape(shp).astype(x.dtype)

def short_conv_mixer(b_gate, c_gate, u, conv_w):
    z = c_gate * u
    n = z.shape[1]
    zp = jnp.pad(z, ((0, 0), (1, 1), (0, 0)))
    conv = zp[:, :n] * conv_w[0] + zp[:, 1:n + 1] * conv_w[1] + zp[:, 2:] * conv_w[2]
    return b_gate * conv

def sdpa(q, k, v):
    B, n, H, d = q.shape
    blk = min(Q_BLOCK, n)
    nb = n // blk
    scale = d ** -0.5

    def one_block(qb):
        s = jnp.einsum('bqhd,bkhd->bhqk', qb, k).astype(jnp.float32) * scale
        p = jax.nn.softmax(s, axis=-1).astype(v.dtype)
        return jnp.einsum('bhqk,bkhd->bqhd', p, v)

    qb = jnp.moveaxis(q.reshape(B, nb, blk, H, d), 1, 0)
    o = lax.map(one_block, qb)
    return jnp.moveaxis(o, 0, 1).reshape(B, n, H * v.shape[-1])

def neighborhood_attention(q, k, v, k_ctx, v_ctx, rpb):
    B, N, H, dh = q.shape
    rows = N // GRID_W
    kh = min(NA_KH, rows)
    scale = dh ** -0.5
    qg, kg, vg = (t.reshape(B, rows, GRID_W, H, dh) for t in (q, k, v))
    r = jnp.arange(rows)
    row_idx = jnp.clip(r - kh // 2, 0, rows - kh)[:, None] + jnp.arange(kh)
    kb, vb = kg[:, row_idx], vg[:, row_idx]
    col = jnp.arange(GRID_W)
    col_start = jnp.clip(col - NA_KW // 2, 0, GRID_W - NA_KW)
    in_window = (col[None, :] >= col_start[:, None]) & (col[None, :] < col_start[:, None] + NA_KW)
    d_row = (row_idx - r[:, None] + NA_KH - 1)[:, None, :, None]
    d_col = jnp.clip(col[None, :] - col[:, None] + NA_KW - 1, 0, 2 * NA_KW - 2)[None, :, None, :]
    bias = rpb[:, d_row, d_col].astype(jnp.float32)
    s_win = jnp.einsum('brqhd,brkchd->bhrqkc', qg, kb).astype(jnp.float32) * scale + bias
    s_win = jnp.where(in_window[:, None, :], s_win, NEG_INF)
    s_ctx = jnp.einsum('brqhd,bhpd->bhrqp', qg, k_ctx).astype(jnp.float32) * scale
    n_win = kh * GRID_W
    s = jnp.concatenate([s_win.reshape(B, H, rows, GRID_W, n_win), s_ctx], axis=-1)
    p = jax.nn.softmax(s, axis=-1).astype(v.dtype)
    p_win = p[..., :n_win].reshape(B, H, rows, GRID_W, kh, GRID_W)
    o = jnp.einsum('bhrqkc,brkchd->brqhd', p_win, vb) + jnp.einsum('bhrqp,bhpd->brqhd', p[..., n_win:], v_ctx)
    return o.reshape(B, N, H * dh)

def fourier_mixer(u, w_fn):
    B, n, _ = u.shape
    ug = u.astype(jnp.float32).reshape(B, n, FN_GROUPS, FN_GROUP_DIM)
    f = jnp.fft.fft2(ug, axes=(1, 3), norm='ortho').real
    return f.reshape(B, n, FN_WIDTH).astype(u.dtype) @ w_fn

def mla_queries(cq, g_q, w_q_up):
    B, n, _ = cq.shape
    q = (rmsnorm(cq, g_q) @ w_q_up).reshape(B, n, MLA_HEADS, MLA_NOPE_DIM + MLA_ROPE_DIM)
    return q[..., :MLA_NOPE_DIM], q[..., MLA_NOPE_DIM:]

def mla_keys_values(ckv_n, k_rope, w_kv_up):
    B, n, _ = ckv_n.shape
    kv = (ckv_n @ w_kv_up).reshape(B, n, MLA_HEADS, MLA_NOPE_DIM + MLA_V_DIM)
    k_r = jnp.broadcast_to(k_rope[:, :, None, :], (B, n, MLA_HEADS, MLA_ROPE_DIM))
    return jnp.concatenate([kv[..., :MLA_NOPE_DIM], k_r], axis=-1), kv[..., MLA_NOPE_DIM:]

def moe_ffn(h, w_router, b_router, w1, w3, w2):
    s = jax.nn.sigmoid((h @ w_router).astype(jnp.float32))
    sb = s + b_router.astype(jnp.float32)
    grp = sb.reshape(sb.shape[:-1] + (N_EXPERT_GROUPS, EXPERTS_PER_GROUP))
    gsel = jnp.argmax(lax.top_k(grp, TOP_K)[0].sum(-1), axis=-1)
    in_group = (jnp.arange(N_EXPERTS) // EXPERTS_PER_GROUP) == gsel[..., None]
    _, idx = lax.top_k(jnp.where(in_group, sb, NEG_INF), TOP_K)
    wsel = jnp.take_along_axis(s, idx, axis=-1)
    wsel = wsel / jnp.sum(wsel, axis=-1, keepdims=True)
    gates = jnp.sum(jax.nn.one_hot(idx, N_EXPERTS, dtype=jnp.float32) * wsel[..., None], axis=-2).astype(h.dtype)
    hid = jax.nn.silu(jnp.einsum('bnd,edf->bnef', h, w1)) * jnp.einsum('bnd,edf->bnef', h, w3)
    return jnp.einsum('bnef,efd->bnd', hid * gates[..., None], w2).astype(h.dtype)

def mixing_context(h, lw):
    B, n, _ = h.shape
    a_b, a_c, a_u, q, k, v, cq, ckv, k_rope, f_u = split_projection(h @ lw['w_in'])
    y_conv = short_conv_mixer(a_b, a_c, a_u, lw['conv_w'])
    q, k, v = (t.reshape(B, n, NA_HEADS, NA_HEAD_DIM) for t in (q, k, v))
    y_na = sdpa(q, k, v)
    q_nope, q_rope = mla_queries(cq, lw['mla_gq'], lw['mla_wq_up'])
    ckv_n = rmsnorm(ckv, lw['mla_gkv'])
    k_m, v_m = mla_keys_values(ckv_n, k_rope, lw['mla_wkv_up'])
    y_mla = sdpa(jnp.concatenate([q_nope, q_rope], axis=-1), k_m, v_m)
    y_fn = fourier_mixer(f_u, lw['w_fn'])
    out = jnp.concatenate([y_conv, y_na, y_mla, y_fn], axis=-1) @ lw['w_out']
    return out, (jnp.swapaxes(k, 1, 2), jnp.swapaxes(v, 1, 2), ckv_n, k_rope)

def mixing_latent(h, lw, na_k_ctx, na_v_ctx, ckv_ctx, krope_ctx, cos, sin):
    B, n, _ = h.shape
    a_b, a_c, a_u, q, k, v, cq, ckv, k_rope, f_u = split_projection(h @ lw['w_in'])
    y_conv = short_conv_mixer(a_b, a_c, a_u, lw['conv_w'])
    q, k, v = (t.reshape(B, n, NA_HEADS, NA_HEAD_DIM) for t in (q, k, v))
    y_na = neighborhood_attention(q, k, v, na_k_ctx, na_v_ctx, lw['na_rpb'])
    q_nope, q_rope = mla_queries(cq, lw['mla_gq'], lw['mla_wq_up'])
    q_rope = apply_axial_rope(q_rope, cos[:, None], sin[:, None])
    k_rope = apply_axial_rope(k_rope, cos, sin)
    k_lat, v_lat = mla_keys_values(rmsnorm(ckv, lw['mla_gkv']), k_rope, lw['mla_wkv_up'])
    k_ctx, v_ctx = mla_keys_values(ckv_ctx, krope_ctx, lw['mla_wkv_up'])
    y_mla = sdpa(jnp.concatenate([q_nope, q_rope], axis=-1),
                 jnp.concatenate([k_lat, k_ctx], axis=1), jnp.concatenate([v_lat, v_ctx], axis=1))
    y_fn = fourier_mixer(f_u, lw['w_fn'])
    return jnp.concatenate([y_conv, y_na, y_mla, y_fn], axis=-1) @ lw['w_out']

def setup_inputs(seed: int = 0) -> dict:
    key = jax.random.key(seed)
    ks = jax.random.split(key, 27)
    nrm = lambda k, shape, s: jax.random.normal(k, shape, jnp.float32) * s
    gain = lambda k, shape: 1.0 + 0.02 * jax.random.normal(k, shape, jnp.float32)
    D = D_MODEL
    return {
        'x_prompt': nrm(ks[0], (BATCH, SEQ, D), 1.0),
        'x_sample': nrm(ks[1], (DEC_BATCH, DEC_SEQ, D), 1.0),
        'cache_na_k': nrm(ks[2], (DEC_BATCH, DEPTH, NA_HEADS, PAST_LEN, NA_HEAD_DIM), 1.0),
        'cache_na_v': nrm(ks[3], (DEC_BATCH, DEPTH, NA_HEADS, PAST_LEN, NA_HEAD_DIM), 1.0),
        'cache_mla_ckv': nrm(ks[4], (DEC_BATCH, DEPTH, PAST_LEN, MLA_KV_LORA), 1.0),
        'cache_mla_krope': nrm(ks[5], (DEC_BATCH, DEPTH, PAST_LEN, MLA_ROPE_DIM), 1.0),
        'c': nrm(ks[6], (DEC_BATCH, D), 1.0),
        'c_ctx': nrm(ks[7], (D,), 1.0),
        'w_ada': nrm(ks[8], (DEPTH, D, 6 * D), 0.5 * D ** -0.5),
        'b_ada': nrm(ks[9], (DEPTH, 6 * D), 0.02),
        'norm1': gain(ks[10], (DEPTH, D)),
        'norm2': gain(ks[11], (DEPTH, D)),
        'w_in': nrm(ks[12], (DEPTH, D, PROJ_WIDTH), D ** -0.5),
        'conv_w': nrm(ks[13], (DEPTH, 3, CONV_WIDTH), 3 ** -0.5),
        'na_rpb': nrm(ks[14], (DEPTH, NA_HEADS, 2 * NA_KH - 1, 2 * NA_KW - 1), 0.5),
        'mla_gq': gain(ks[15], (DEPTH, MLA_Q_LORA)),
        'mla_wq_up': nrm(ks[16], (DEPTH, MLA_Q_LORA, MLA_HEADS * (MLA_NOPE_DIM + MLA_ROPE_DIM)), MLA_Q_LORA ** -0.5),
        'mla_gkv': gain(ks[17], (DEPTH, MLA_KV_LORA)),
        'mla_wkv_up': nrm(ks[18], (DEPTH, MLA_KV_LORA, MLA_HEADS * (MLA_NOPE_DIM + MLA_V_DIM)), MLA_KV_LORA ** -0.5),
        'w_fn': nrm(ks[19], (DEPTH, FN_WIDTH, FN_WIDTH), FN_WIDTH ** -0.5),
        'w_out': nrm(ks[20], (DEPTH, MIX_WIDTH, D), MIX_WIDTH ** -0.5),
        'w_router': nrm(ks[21], (D, N_EXPERTS), D ** -0.5),
        'b_router': nrm(ks[22], (N_EXPERTS,), 0.01),
        'w1': nrm(ks[23], (DEPTH, N_EXPERTS, D, EXPERT_FF), D ** -0.5),
        'w3': nrm(ks[24], (DEPTH, N_EXPERTS, D, EXPERT_FF), D ** -0.5),
        'w2': nrm(ks[25], (DEPTH, N_EXPERTS, EXPERT_FF, D), EXPERT_FF ** -0.5),
        'norm_f': gain(ks[26], (D,)),
    }

def reference(x_prompt, x_sample, cache_na_k, cache_na_v, cache_mla_ckv, cache_mla_krope, c, c_ctx,
              w_ada, b_ada, norm1, norm2, w_in, conv_w, na_rpb, mla_gq, mla_wq_up, mla_gkv, mla_wkv_up,
              w_fn, w_out, w_router, b_router, w1, w3, w2, norm_f):
    def layer_weights(l):
        return {'w_in': w_in[l], 'conv_w': conv_w[l], 'na_rpb': na_rpb[l], 'mla_gq': mla_gq[l],
                'mla_wq_up': mla_wq_up[l], 'mla_gkv': mla_gkv[l], 'mla_wkv_up': mla_wkv_up[l],
                'w_fn': w_fn[l], 'w_out': w_out[l]}

    xp = x_prompt
    st_k, st_v, st_ckv, st_kr = [], [], [], []
    for l in range(DEPTH):
        lw = layer_weights(l)
        sh1, sc1, g1, sh2, sc2, g2 = ada_modulation(c_ctx[None, :], w_ada[l], b_ada[l])
        mix, (nk, nv, nckv, nkr) = mixing_context(modulate(xp, norm1[l], sh1, sc1), lw)
        xp = xp + g1 * mix
        xp = xp + g2 * moe_ffn(modulate(xp, norm2[l], sh2, sc2), w_router, b_router, w1[l], w3[l], w2[l])
        st_k.append(nk)
        st_v.append(nv)
        st_ckv.append(nckv)
        st_kr.append(nkr)
    y_prompt = rmsnorm(xp, norm_f)
    new_na_k = jnp.stack(st_k, axis=1)
    new_na_v = jnp.stack(st_v, axis=1)
    new_mla_ckv = jnp.stack(st_ckv, axis=1)
    new_mla_krope = jnp.stack(st_kr, axis=1)

    cos, sin = axial_rope_tables(x_sample.shape[1])
    xs = x_sample
    for l in range(DEPTH):
        lw = layer_weights(l)
        sh1, sc1, g1, sh2, sc2, g2 = ada_modulation(c, w_ada[l], b_ada[l])
        mix = mixing_latent(modulate(xs, norm1[l], sh1, sc1), lw, cache_na_k[:, l], cache_na_v[:, l],
                            cache_mla_ckv[:, l], cache_mla_krope[:, l], cos, sin)
        xs = xs + g1 * mix
        xs = xs + g2 * moe_ffn(modulate(xs, norm2[l], sh2, sc2), w_router, b_router, w1[l], w3[l], w2[l])
    y_sample = rmsnorm(xs, norm_f)
    return (y_prompt, y_sample, new_na_k, new_na_v, new_mla_ckv, new_mla_krope)


_drawn_inputs = setup_inputs


def setup_inputs(seed=0):
    import zlib

    import numpy as np

    out = dict(_drawn_inputs(seed))
    spreads = {}
    factors = {'cache_mla_ckv': 3.506,
     'cache_mla_krope': 8.0,
     'mla_gq': 8.0,
     'mla_gkv': 3.046,
     'norm_f': 2.793}
    for name, (base, spread) in spreads.items():
        noise = np.random.default_rng([zlib.crc32(name.encode()), seed]).standard_normal(out[name].shape)
        drawn = base * np.exp(spread * noise) if base else spread * noise
        out[name] = __import__('jax').numpy.asarray(drawn.astype(out[name].dtype))
    for name, factor in factors.items():
        out[name] = (out[name] * factor).astype(out[name].dtype)
    return out
```

```python
from contextlib import ExitStack

import numpy as np

import concourse.bass as bass
from concourse import mybir

F32 = mybir.dt.float32
I32 = mybir.dt.int32
ALU = mybir.AluOpType
ACT = mybir.ActivationFunctionType
AX = mybir.AxisListType

P = 128
DEPTH = 2
D = 1024
KD = D // P
N_LAT = 512
N_CTX = 128
N_TOK = N_LAT + N_CTX
GRID_W = 64
GRID_H = N_LAT // GRID_W
TL = N_LAT // P
TT = N_TOK // P
HEADS = 4
HD = 64
NK = 16
N_DR = 15
N_DC = 31
ROPE = 32
QK = HD + ROPE
NE = 16
FF = 256
EPS = 1e-6
MASKED = -1e30
CREDIT = 2
DVE_CHAIN = 108
BANK = 512
SLOT = 2048
RING = 6

WIN = [0, 64, 192, 256]
BIAS_KIND = [0, 1, 1, 2]
WIN_V = [(0, 1), (6, 7), (7, 8), (2, 3)]
TAB_W = 64
OFF0 = 16


class Signal:

    def __init__(self, sem, per_layer):
        self.sem, self.per_layer = sem, per_layer

    def at(self, layer, n):
        return layer * self.per_layer + n


class PsumPlan:

    def __init__(self):
        self.copies, self.where, self.copied_at, self.cursor, self.count = {}, {}, {}, 0, 0
        self.freed = [0] * 8
        self.last = [None] * 8

    def add(self, key, banks=1, drains=1):
        if banks == 2 and self.cursor % 2:
            self.cursor += 1
        b = self.cursor % 8
        waits = {}
        for c in range(b, b + banks):
            if self.last[c] is not None:
                sem, value = self.last[c]
                waits[sem] = max(waits.get(sem, 0), value)
            else:
                waits[c] = waits.get(c, 0)
                waits[c - c % 2] = waits.get(c - c % 2, 0)
        self.freed[b] += drains
        self.copies[key] = drains
        for c in range(b, b + banks):
            self.last[c] = (b, self.freed[b])
        self.cursor += banks
        self.count += 1
        self.where[key] = (self.count, b, banks, waits)
        self.copied_at[key] = self.freed[b]


def attention_units():
    units = [("na", h, t) for t in range(TL) for h in range(HEADS)]
    units += [("nac", h, TL) for h in range(HEADS)]
    units += [("mlc", h, TL) for h in range(HEADS)]
    units += [("ml", h, t) for h in range(HEADS) for t in range(TL)]
    return units


UNITS = attention_units()
WIDTH = {"na": 384, "nac": 128, "mlc": 128, "ml": 640}


def output_after(u):
    kind, h, t = UNITS[u]
    if kind == "ml":
        return ("mlO", h // 2, 0) if h % 2 and t == TL - 1 else None
    return (kind + "O", h // 2, t) if h % 2 else None


def psum_plan():
    plan = PsumPlan()
    for g in range(3):
        plan.add(("ada", g))
        if g == 0:
            plan.add("modT")
    for k in range(KD):
        plan.add(("h1T", k), 2, 2)
    for m in range(10):
        plan.add(("pT", m), 2)
    for t in range(TT):
        plan.add(("pN", t), 2, 2)
    for cs in range(2):
        plan.add(("fnw", cs))
    for ch in range(2):
        for cs in range(2):
            plan.add(("fnA", ch, cs), 2)
    for kk in range(2):
        plan.add(("cqT", kk), 2)
    plan.add("ckT", 2)
    plan.add("krT", 2, 2)
    for p in range(2):
        plan.add(("kup", p), 2)
    for o in range(2):
        plan.add(("fnY", o), 2)
    for j in range(3):
        plan.add(("vup", j))
    for t in range(TT + 1):
        if t < TT:
            plan.add(("qup", t))
        if t:
            plan.add(("qT", t - 1))
    for step in range(len(UNITS) + 3):
        for what, u in steps_at(step):
            kind = UNITS[u][0]
            if what == "S":
                plan.add(("S", u), 2 if kind == "ml" else 1)
            elif what == "T":
                plan.add(("T", u), 2 if kind == "ml" else 1)
            else:
                plan.add(output_after(u))
    for t in range(TT):
        plan.add(("out", t), 2)
    for k in range(KD):
        plan.add(("h2T", k), 2, 2)
    plan.add("rl", 2)
    plan.add("rT", 2)
    plan.add("rank")
    return plan


def steps_at(step):
    out = []
    if step < len(UNITS):
        out.append(("S", step))
    if 0 <= step - 2 < len(UNITS):
        out.append(("T", step - 2))
    if 0 <= step - 3 < len(UNITS) and output_after(step - 3):
        out.append(("O", step - 3))
    return out


PROJ_T = ["c0", "u0", "b0", "c1", "u1", "b1", "q0", "q1", "k0", "k1"]
CHUNKS = [("ada", g, k) for g in range(3) for k in range(KD)] + [("wT", m) for m in range(5)] \
    + [("wN", c) for c in range(4)] + [("wO", c) for c in range(4)]
CHUNK_AT = {c: n for n, c in enumerate(CHUNKS)}
NCH = len(CHUNKS)
SLOT_LOADS = [len(range(s, NCH, RING)) for s in range(RING)]
X13 = [1, 4]
X2 = [3, 0]


def mixer_kernel(nc, A, O):
    plan = psum_plan()
    ctx = ExitStack()
    with ctx:
        top = [0]

        def cut(n):
            top[0] += n
            return top[0] - n

        ARENA = 53060
        arena = ctx.enter_context(nc.sbuf_tensor("arena", [P, ARENA], F32))

        def view(at, *shape, parts=P, p0=0):
            n = int(np.prod(shape))
            v = arena[p0:p0 + parts, at:at + n]
            if len(shape) == 2:
                return v.rearrange("p (a b) -> p a b", a=shape[0])
            if len(shape) == 3:
                return v.rearrange("p (a b c) -> p a b c", a=shape[0], b=shape[1])
            return v

        def ints(name, *shape):
            return ctx.enter_context(nc.sbuf_tensor(name, [P, *shape], I32))

        x = view(cut(TT * D), TT, D)
        at_h = cut(KD * N_TOK)
        hT = view(at_h, KD, N_TOK)
        probsT = view(at_h, 2, 5, N_LAT)
        probsT_s = view(at_h, 4, 3, P)
        h2 = view(at_h, TT, D)
        at_y = cut(KD * N_TOK)
        xn = view(at_y, TT, D)
        yT = view(at_y, KD, N_TOK)
        h2T = view(at_y, KD, N_TOK)
        at_ring = cut(RING * SLOT)
        slot = [view(at_ring + s * SLOT, SLOT) for s in range(RING)]

        def ring(s, *shape, slots=1):
            return view(at_ring + s * SLOT, *shape)

        ident = view(cut(P), P)
        before = view(cut(P), P)
        ones = view(cut(P), P)
        chan = view(cut(2 * P), 2, P)
        rope = view(cut(2 * TL * 16), 2, TL, 16)
        cond = view(cut(KD * 32), KD, 32)
        w_r = view(cut(KD * 32), KD, 32)
        b_r = view(cut(NE), NE)
        iota16 = view(cut(NE), NE)
        count16 = view(cut(NE), NE)
        count4 = view(cut(4), 4)
        minus_half = view(cut(1), 1)
        limits = view(cut(4), 4)
        n1c = view(cut(KD), KD)
        mod_s = view(cut(2 * KD), 2, KD)
        mod_a = view(cut(2 * KD), 2, KD)
        convw = view(cut(6), 2, 3)
        gq = view(cut(2), 2)
        gkv = view(cut(P), P)
        stat = view(cut(5 * TT), 5, TT)
        rstd = view(cut(5 * TT), 5, TT)
        rowmax = view(cut(4), 4)
        negmax = view(cut(4), 4)
        rowsum = view(cut(4), 4)
        rowinv = view(cut(4), 4)
        gates = view(cut(2 * TT), 2, TT)
        at_a = cut(2 * TL * N_LAT + 2 * P)
        dft = view(at_a, 2, TL, N_LAT)
        dft_c = view(at_a + 2 * TL * N_LAT, 2, P)
        k_m = view(at_a, HEADS, 768)
        cqT = view(at_a + HEADS * 768, 2, N_TOK)
        at_b = cut(4 * N_TOK)
        dftT = view(at_b, 2, 2, N_TOK)
        q_m = view(at_b, HEADS, N_TOK)
        hs = view(at_b, 2, D)
        at_c = cut(2720)
        nat = view(at_c, TT, 512)
        c_sb = view(at_c, N_TOK)
        z_lat = view(at_c + 640, 528)
        z_ctx = view(at_c + 1168, 130)
        cv = view(at_c + 1298, N_TOK)
        masks = view(at_c + 1940, 3, 256)
        probs = view(at_c, 3, 640)
        junk = view(at_c, D)
        hsT_at = at_c
        hid = view(at_c + 2048, 2, FF)
        at_d = cut(HEADS * N_TOK + 2 * 768 + 9 * 256)
        q_n = view(at_d, HEADS, N_TOK)
        k_n = view(at_d + HEADS * N_TOK, 2, 768)
        v_n = view(at_d + HEADS * N_TOK + 2 * 768, 9, 256)
        mods = view(at_d, 3, 512)
        b_ada = view(at_d + 1536, 3, 512)
        n2q = view(at_d + 3072, 512)
        rows = view(at_d, 3, 2, D)
        at_g = cut(HEADS * 3 * 256)
        bias = view(at_g, HEADS, 3, 256)
        ys = view(at_g, 2, D)
        ff_t = view(at_g + 2 * D, 2, FF)
        at_v = cut(6 * 256)
        w_fn = view(at_v, 2, 256)
        wf = view(at_v + 512, 2, 2, 256)
        v_m = view(at_v, 6, 256)
        ckv_n = view(cut(TT * P), TT, P)
        kr = view(cut(TT * ROPE), TT, ROPE)
        ckvT = view(cut(768), 768)
        wq_up = view(cut(768), 2, 384)
        wkv_up = view(cut(512), 512)
        hidT = wq_up[:, 0, 0:256].rearrange("p (a b) -> p a b", a=2)
        hsT = [view(hsT_at, KD, P), view(hsT_at + KD * P, KD, P)]
        q_up = view(at_c, 2, 384)
        tmp4 = view(cut(4 * 64), 4, 64)
        sq_junk = tmp4.rearrange("p a b -> p (a b)")
        c_raw = view(at_g, KD, 2)
        c_exp = view(at_g + 2 * KD, KD, 2)
        zeros = view(at_g + D, D)
        normf_row = view(at_c + D, D)
        r_at = [at_g]

        def rcut(*shape):
            r_at[0] += int(np.prod(shape))
            return view(r_at[0] - int(np.prod(shape)), *shape)

        r_log = rcut(N_TOK)
        r_z = rcut(TT, NE)
        r_s = rcut(TT, NE)
        r_sb = rcut(TT, NE)
        r_pair = rcut(TT * 4, 6)
        r_g = rcut(TT, 4)
        r_gm = rcut(TT)
        r_first = rcut(TT, 4)
        r_m = rcut(TT, NE)
        r_t = rcut(TT, NE)
        r_sel = rcut(2, TT, NE)
        r_mask = rcut(TT, NE)
        r_w = rcut(2, TT)
        r_cum = rcut(TT + 1, NE)
        r_rank = rcut(TT, NE)
        r_pos = rcut(2, TT)
        r_n = rcut(8)
        assert r_at[0] <= at_g + HEADS * 3 * 256, r_at[0] - at_g
        assert top[0] <= ARENA, top[0]
        pos_i = ints("pos_i", 2 * TT)
        rounds_i = ints("rounds_i", 1)
        list_i = ints("list_i", NE, 2)
        idx_i = ints("idx_i", 2)
        out_i = ints("out_i", 2)
        tok_i = ints("tok_i", 2, TT, 2)
        none_i = ints("none_i", 2, 2)

        ps = ctx.enter_context(nc.psum_tensor("ps", [P, 8 * BANK], F32))

        tab = nc.dram_tensor("bias_tab", (HEADS, GRID_H, TAB_W, GRID_H), F32, kind="Internal").ap()
        bias_d = nc.dram_tensor("bias_rows", (P // GRID_H, HEADS, GRID_H, 3, 256), F32, kind="Internal").ap()
        mod_d = nc.dram_tensor("mod_rows", (2, 6 * D), F32, kind="Internal").ap()
        h_d = nc.dram_tensor("expert_in", (N_TOK + 1, D), F32, kind="Internal").ap()
        list_d = nc.dram_tensor("expert_list", (N_TOK * NE, 2), I32, kind="Internal").ap()
        y_d = nc.dram_tensor("expert_out", (2 * N_TOK + 2, D), F32, kind="Internal").ap()
        y_by = y_d[0:2 * N_TOK, :].rearrange("(t p a) d -> t a p d", p=P, a=2)

        def sem(name):
            return ctx.enter_context(nc.semaphore(name))

        def per_layer(name, n):
            return Signal(sem(name), n)

        psum_full = per_layer("psum_full", plan.count)
        psum_copied = [per_layer(f"psum_copied{b}", plan.freed[b]) for b in range(8)]
        chunk_in = [per_layer(f"chunk_in{s}", 16 * SLOT_LOADS[s]) for s in range(RING)]
        chunk_used = per_layer("chunk_used", 3 * (KD - 1))
        const_in = sem("const_in")
        x_in = sem("x_in")
        passed = sem("passed")
        router_in = sem("router_in")
        dft_in = per_layer("dft_in", 32)
        ada_in = per_layer("ada_in", 16 * 8)
        small_in = per_layer("small_in", 16 * 6)
        kv_cache_in = per_layer("kv_cache_in", 16 * 2)
        tab_in = per_layer("tab_in", 16 * GRID_H)
        table_zero = sem("table_zero")
        skewed = per_layer("skewed", 16 * 3)
        bias_in = per_layer("bias_in", 16 * (1 + HEADS))
        krope_in = per_layer("krope_in", 16 * HEADS)
        bias_ready = per_layer("bias_ready", 1)
        cond_exp = sem("cond_exp")
        cond_ready = sem("cond_ready")
        setup_done = sem("setup_done")
        mods_scaled = per_layer("mods_scaled", 1)
        mods_out = per_layer("mods_out", 16 * 4)
        gate1_in = per_layer("gate1_in", 16 * 2)
        mod2_in = per_layer("mod2_in", 16 * 4)
        gate2_in = per_layer("gate2_in", 16 * 2)
        squares = per_layer("squares", TT)
        root_x, root_q, root_kv, root_mixed = (per_layer(n, TT) for n in ("root_x", "root_q", "root_kv", "root_mixed"))
        eps_added = sem("eps_added")
        xn_ready = per_layer("xn_ready", TT)
        q_zeroed = per_layer("q_zeroed", 1)
        v_shifted = per_layer("v_shifted", 32)
        kv_squares = per_layer("kv_squares", 2 * TT)
        ckv_raw = per_layer("ckv_raw", TT)
        ckv_ready = per_layer("ckv_ready", TT)
        kr_ready = per_layer("kr_ready", 1)
        caches_out = per_layer("caches_out", 16 * 4)
        q_up_ready = per_layer("q_up_ready", TT)
        NU = len(UNITS)
        max_ready = per_layer("max_ready", NU)
        exp_ready = per_layer("exp_ready", sum(kind == "na" for kind, _, _ in UNITS))
        inv_ready = per_layer("inv_ready", NU)
        probs_ready = per_layer("probs_ready", NU)
        x_mixed = per_layer("x_mixed", TT)
        squares2 = per_layer("squares2", TT)
        h2_scaled = per_layer("h2_scaled", TT)
        h2_ready = per_layer("h2_ready", TT)
        h2_out = per_layer("h2_out", 16 * TT)
        rexp_ready = per_layer("rexp_ready", 1)
        mask_ready = per_layer("mask_ready", 1)
        routed = per_layer("routed", 1)
        scattered = per_layer("scattered", 16 * 2 * TT)
        list_zeroed = sem("list_zeroed")
        yg_in = [per_layer(f"yg_in{b}", 32 * ((TT + 1 - b) // 2)) for b in range(2)]
        y_first = per_layer("y_first", TT)
        x_done = per_layer("x_done", TT)
        logits_ready = per_layer("logits_ready", 1)
        cond_step = sem("cond_step")
        final_squares = sem("final_squares")
        final_root = sem("final_root")
        y_final = sem("y_final")
        y_out = sem("y_out")
        normf_in = sem("normf_in")
        list_in = sem("list_in")
        list_used = sem("list_used")
        idx_ready = sem("idx_ready")
        place_ready = sem("place_ready")
        hs_in = [sem(f"hs_in{b}") for b in range(2)]
        hsT_full = sem("hsT_full")
        hsT_ready = sem("hsT_ready")
        up_full = sem("up_full")
        e_ready = sem("e_ready")
        hidT_ready = sem("hidT_ready")
        silu_chain = sem("silu_chain")
        hid_ready = sem("hid_ready")
        hidT_full = sem("hidT_full")
        dn_full = sem("dn_full")
        ys_low = sem("ys_low")
        ys_high = sem("ys_high")
        ys_out = [sem(f"ys_out{b}") for b in range(2)]
        x13_in = [sem(f"x13_in{b}") for b in range(2)]
        x2_in = [sem(f"x2_in{b}") for b in range(2)]
        dve_chain = per_layer("dve_chain", DVE_CHAIN)

        block = ctx.enter_context(nc.Block())

        def wait(eng, sem, value):
            eng.wait_ge(sem, value)
            if eng is nc.gpsimd or eng is nc.sync:
                eng.sem_inc(passed, 1)

        def acquire(pe, l, key):
            _, b, banks, waits = plan.where[key]
            for s, value in waits.items():
                pe.wait_ge(psum_copied[s].sem, psum_copied[s].at(l, value))
            return ps[:, b * BANK:(b + banks) * BANK]

        def place(key):
            _, b, banks, _ = plan.where[key]
            return ps[:, b * BANK:(b + banks) * BANK]

        def filled(eng, l, key):
            n, b, banks, _ = plan.where[key]
            wait(eng, psum_full.sem, psum_full.at(l, n))
            return ps[:, b * BANK:(b + banks) * BANK]

        copies = {}

        def bank_of(key):
            copies[key] = copies.get(key, 0) + 1
            return psum_copied[plan.where[key][1]].sem

        def copied(eng, l, *keys):
            need = {}
            for key in keys:
                _, b, _, _ = plan.where[key]
                need[b] = max(need.get(b, 0), plan.copied_at[key])
            for b, value in need.items():
                wait(eng, psum_copied[b].sem, psum_copied[b].at(l, value))
            if eng is nc.tensor:
                eng.sem_inc(passed, 1)

        def used(eng, l, n):
            kind, *i = CHUNKS[n]
            if kind == "ada" and i[1] < KD - 1:
                wait(eng, chunk_used.sem, chunk_used.at(l, i[0] * (KD - 1) + i[1] + 1))
            else:
                filled(eng, l, {"ada": ("ada", i[0]), "wT": ("pT", 2 * i[0] + 1), "wN": ("pN", TT - 1),
                                "wO": ("out", TT - 1)}[kind])

        def chunk_wait(pe, l, chunk):
            n = CHUNK_AT[chunk]
            s = n % RING
            pe.wait_ge(chunk_in[s].sem, chunk_in[s].at(l, 16 * (n // RING + 1)))
            return at_ring + s * SLOT

        def by_head(ap, h):
            return ap[:, h * HD:(h + 1) * HD]

        @block.sync
        def _(sp):
            for n, (dst, src) in enumerate([(ident, A["c_ident"]), (before, A["c_before"]), (ones, A["c_ones"]),
                                            (chan, A["c_chan"]), (rope, A["c_rope"]), (b_r, A["b_router"]),
                                            (iota16, A["c_iota"]), (count16, A["c_count"]),
                                            (count4, A["c_count"]), (limits, A["c_limits"])]):
                if n == 5:
                    src = src.rearrange("(a e) -> a e", a=1).broadcast_to((P, NE))
                if n == 8:
                    src = src[:, NE - 4:NE]
                sp.dma_start(dst, src).then_inc(const_in, 16)
            sp.dma_start(tok_i[:, :, :, :], A["c_tok"]).then_inc(const_in, 16)
            for t in range(TT):
                sp.dma_start(x[:, t, :], A["x_all"][t * P:(t + 1) * P, :]).then_inc(x_in, 16)
            sp.dma_start(c_raw, A["c_cols"]).then_inc(x_in, 16)
            done = sp.alloc_register("experts_done_sp")
            sp.reg_mov(done, 0)
            with sp.Fori(0, DEPTH) as l:
                for n, chunk in enumerate(CHUNKS):
                    s = n % RING
                    if n == 0:
                        wait(sp, dn_full, sp.snap(done, min_val=0, max_val=160) + CREDIT)
                    elif n >= RING:
                        used(sp, l, n - RING)
                    kind, i = chunk[0], chunk[1]
                    dst = slot[s]
                    if kind == "ada":
                        src = A["w_ada"][bass.ds(l, 1), chunk[2] * P:(chunk[2] + 1) * P, i * SLOT:(i + 1) * SLOT]
                        src = src.rearrange("a p n -> (a p) n")
                    elif kind == "wT":
                        src = A["w_t"][bass.ds(l, 1), i].rearrange("a p n -> (a p) n")
                    elif kind == "wN":
                        dst = view(at_ring + s * SLOT, 2 * 928)
                        src = A["w_n"][bass.ds(l, 1), i].rearrange("a p n -> (a p) n")
                    else:
                        dst = ring(s, 2, D)
                        src = A["w_out"][bass.ds(l, 1), i * 2 * P:(i + 1) * 2 * P, :]
                        src = src.rearrange("a (k p) n -> p (a k) n", p=P)
                    sp.dma_start(dst, src).then_inc(chunk_in[s].sem, 16)
                    if chunk == ("ada", 2, KD - 1):
                        sp.dma_start(view(at_a, 2 * TL * N_LAT), A["c_dft"]).then_inc(dft_in.sem, 16)
                        sp.dma_start(view(at_a + 2 * TL * N_LAT, 2 * P), A["c_dft_ctx"]).then_inc(dft_in.sem, 16)
                used(sp, l, NCH - 1)

                def load_expert(r, i, b):
                    base = sp.snap(done, min_val=0, max_val=160)
                    e = 2 * i + b
                    wait(sp, up_full, base + e + 1)
                    for half in range(2):
                        sp.dma_start(view(at_ring + (X13[b] + half) * SLOT, SLOT),
                                     A["w_13"][bass.ds(l, 1), bass.ds(e, 1), :, half * SLOT:(half + 1) * SLOT]
                                     .rearrange("a b p n -> (a b p) n")).then_inc(x13_in[b], 16)
                    wait(sp, dn_full, base + e + 1)
                    sp.dma_start(ring(X2[b], 2, D), A["w2"][bass.ds(l, 1), bass.ds(e, 1), :, :]
                                 .rearrange("a b (k p) n -> p (a b k) n", p=P)).then_inc(x2_in[b], 16)

                def expert_rounds():
                    wait(sp, routed.sem, routed.at(l, 1))
                    n_rounds = sp.value_load(rounds_i[0:1, 0:1], min_val=1, max_val=5)
                    with sp.Fori(0, n_rounds) as r:
                        with sp.Fori(0, NE // 2) as i:
                            for b in range(2):
                                load_expert(r, i, b)
                        sp.reg_add(done, done, NE)
                expert_rounds()
            wait(sp, x_done.sem, x_done.at(DEPTH, 0))
            sp.dma_start(normf_row, A["norm_f"].broadcast_to((P, D))).then_inc(normf_in, 16)
            wait(sp, y_out, 16 * TT)
            wait(sp, caches_out.sem, caches_out.at(DEPTH, 0))

        @block.gpsimd
        def _(pool):
            pool.memset(w_r, 0.0).then_inc(setup_done, 1)
            pool.memset(none_i[:, :, 0], N_TOK).then_inc(setup_done, 1)
            for b in range(2):
                pool.memset(none_i[:, b, 1:2], 2 * N_TOK + b).then_inc(setup_done, 1)
            pool.memset(minus_half, -0.5)
            pool.memset(zeros, 0.0).then_inc(setup_done, 1)
            pool.wait_ge(setup_done, 5)
            pool.dma_start(w_r[:, :, 0:NE], A["w_router"].rearrange("(k p) e -> p k e", p=P)).then_inc(router_in, 16)
            pool.dma_start(h_d[N_TOK:N_TOK + 1, :], zeros[0:1, :]).then_inc(list_zeroed, 16)

            def empty_lists():
                pool.dma_start(list_d.rearrange("(p n e) a -> p n e a", p=P, e=2),
                               none_i[:, :, :].unsqueeze(1).broadcast_to((P, N_TOK * NE // P // 2, 2, 2)))\
                    .then_inc(list_zeroed, 16)
            empty_lists()
            pool.dma_start(tab.rearrange("h r c k -> (h r) (c k)"), zeros[0:32, 0:TAB_W * GRID_H])\
                .then_inc(table_zero, 16)
            pool.wait_ge(table_zero, 16)
            pool.wait_ge(list_zeroed, 32)
            pool.wait_ge(cond_ready, 1)
            done = pool.alloc_register("experts_done_pool")
            pool.reg_mov(done, 0)

            def inverse_root(n, i, t, root):
                pool.tensor_scalar(stat[:, i, t:t + 1], stat[:, i, t:t + 1], EPS, None, ALU.add).then_inc(eps_added, 1)
                pool.wait_ge(eps_added, n)
                pool.sem_inc(passed, 1)
                pool.tensor_tensor(rstd[:, i, t:t + 1], stat[:, i, t:t + 1], minus_half, ALU.pow).then_inc(root, 1)

            with pool.Fori(0, DEPTH) as l:
                for t in range(TT):
                    wait(pool, squares.sem, squares.at(l, t + 1))
                    inverse_root(l * 4 * TT + t + 1, 0, t, root_x.sem)
                wait(pool, x_done.sem, x_done.at(l, 0))

                def row(a, lo, n, parts):
                    return a[bass.ds(l, 1), lo:lo + n].broadcast_to((parts, n))

                for j in range(4):
                    for g in range(3):
                        if g == 0:
                            pool.dma_start(b_ada[32 * j:32 * j + 32, :, :],
                                           A["b_ada_q"][bass.ds(l, 1), j].broadcast_to((32, 3, 512)))\
                                .then_inc(ada_in.sem, 16)
                for j in range(2):
                    pool.dma_start(n2q[32 * j:32 * j + 32, :], row(A["norm2"], 512 * j, 512, 32)).then_inc(ada_in.sem, 16)
                pool.dma_start(n1c, A["norm1_c"][bass.ds(l, 1)].rearrange("a p k -> (a p) k")).then_inc(ada_in.sem, 16)
                pool.dma_start(convw, A["conv_c"][bass.ds(l, 1)].rearrange("a p c w -> (a p) c w")).then_inc(ada_in.sem, 16)
                for r in range(GRID_H):
                    pool.dma_start(tab[:, r, OFF0:OFF0 + N_DC, :],
                                   A["rpb_t"][bass.ds(l, 1), :, :, GRID_H - 1 - r:2 * GRID_H - 1 - r]
                                   .rearrange("a h c k -> (a h) c k")).then_inc(tab_in.sem, 16)
                pool.dma_start(masks, A["c_masks"]).then_inc(bias_in.sem, 16)
                pool.dma_start(gq, A["gq_c"][bass.ds(l, 1)].rearrange("a p k -> (a p) k")).then_inc(small_in.sem, 16)
                pool.dma_start(gkv, row(A["mla_gkv"], 0, P, P)).then_inc(small_in.sem, 16)
                pool.dma_start(w_fn, A["w_fn"][bass.ds(l, 1)].rearrange("a (k p) n -> p (a k) n", p=P)).then_inc(small_in.sem, 16)
                pool.dma_start(wq_up, A["mla_wq_up"][bass.ds(l, 1)].rearrange("a (k p) n -> p (a k) n", p=P)).then_inc(small_in.sem, 16)
                pool.dma_start(wkv_up, A["mla_wkv_up"][bass.ds(l, 1)].rearrange("a p n -> (a p) n")).then_inc(small_in.sem, 16)
                pool.dma_start(ckvT[:, 512:640], A["ckv_t"][bass.ds(l, 1)].rearrange("a p n -> (a p) n")).then_inc(small_in.sem, 16)
                wait(pool, tab_in.sem, tab_in.at(l, 16 * GRID_H))
                for kind in range(3):
                    first = OFF0 + 15 - 8 * kind
                    src = bass.AP(tensor=tab.tensor, offset=first * GRID_H,
                                  ap=[[GRID_H * TAB_W * GRID_H, HEADS], [TAB_W * GRID_H, GRID_H], [-GRID_H, 16], [1, 256]])
                    pool.dma_start(bias_d[:, :, :, kind, :].rearrange("c h r n -> h r c n"), src)\
                        .then_inc(skewed.sem, 16)
                wait(pool, skewed.sem, skewed.at(l, 16 * 3))
                for h in range(HEADS):
                    pool.dma_start(bias[:, h, :, :], bias_d[:, h].rearrange("c r k n -> c r (k n)")).then_inc(bias_in.sem, 16)
                wait(pool, bias_in.sem, bias_in.at(l, bias_in.per_layer))
                for h in range(HEADS):
                    ins = pool.tensor_tensor(bias[:, h, :, :], bias[:, h, :, :], masks, ALU.add)
                ins.then_inc(bias_ready.sem, 1)
                for j in range(4):
                    if j == 0:
                        copied(pool, l, ("ada", 0), ("ada", 1), ("ada", 2))
                        wait(pool, mods_scaled.sem, mods_scaled.at(l, 1))
                    pool.dma_start(mod_d.rearrange("c (g j n) -> c g j n", g=3, j=4)[:, :, j, :],
                                   mods[32 * j:32 * j + 32:16, :, :]).then_inc(mods_out.sem, 16)
                wait(pool, mods_out.sem, mods_out.at(l, 64))
                copied(pool, l, "modT")
                pool.memset(q_n, 0.0).then_inc(q_zeroed.sem, 1)
                wait(pool, q_zeroed.sem, q_zeroed.at(l, 1))
                pool.dma_start(k_n[:, :, 512:640], A["nk_t"][bass.ds(l, 1)].rearrange("a p k n -> (a p) k n")).then_inc(kv_cache_in.sem, 16)
                pool.dma_start(v_n[:, 5, :], A["nv_t"][bass.ds(l, 1)].rearrange("a p n -> (a p) n")).then_inc(kv_cache_in.sem, 16)
                for t in range(TT):
                    wait(pool, kv_squares.sem, kv_squares.at(l, 2 * t + 2))
                    inverse_root(l * 4 * TT + TT + 2 * t + 1, 1, t, root_q.sem)
                    inverse_root(l * 4 * TT + TT + 2 * t + 2, 2, t, root_kv.sem)
                copied(pool, l, *[("pN", t) for t in range(TT)])
                pool.dma_start(v_n[0:64, 6:9, :], v_n[64:128, 0:3, :]).then_inc(v_shifted.sem, 16)
                pool.dma_start(v_n[64:128, 6:9, :], v_n[0:64, 1:4, :]).then_inc(v_shifted.sem, 16)
                copied(pool, l, ("pT", 8), ("pT", 9))
                wait(pool, ckv_ready.sem, ckv_ready.at(l, TT))
                wait(pool, kr_ready.sem, kr_ready.at(l, 1))
                for n, (dst, src) in enumerate([(O["nk"], k_n[:, :, 640:768]), (O["nv"], v_n[:, 4, :]),
                                                (O["ckv"], ckv_n[:, TL, :]), (O["kr"], kr[:, TL, :])]):
                    dst = dst[bass.ds(l, 1)]
                    dst = dst.rearrange("a p k n -> (a p) k n") if n == 0 else dst.rearrange("a p n -> (a p) n")
                    pool.dma_start(dst, src).then_inc(caches_out.sem, 16)
                filled(pool, l, ("fnA", 1, 1))
                for h in range(HEADS):
                    pool.dma_start(k_m[64:96, h, 512:640], A["krope_t"][bass.ds(l, 1)].rearrange("a p n -> (a p) n")).then_inc(krope_in.sem, 16)
                for u, (kind, h, t) in enumerate(UNITS):
                    wait(pool, inv_ready.sem, inv_ready.at(l, u + 1))
                    pr = probs[:, u % 3, 0:WIDTH[kind]]
                    pool.tensor_scalar(pr, pr, rowinv[:, u % 4:u % 4 + 1], None, ALU.mult).then_inc(probs_ready.sem, 1)
                    if 22 <= u < 28:
                        wait(pool, caches_out.sem, caches_out.at(l, 64))
                        filled(pool, l, ("nacO", 1, TL))
                        n, c = divmod(u - 22, 2)
                        lo = [2 * D, 4 * D, 3 * D][n]
                        pool.dma_start(rows[:, n, c, :], mod_d[c:c + 1, lo:lo + D].broadcast_to((P, D)))\
                            .then_inc((gate1_in if n == 0 else mod2_in).sem, 16)
                for t in range(TT):
                    wait(pool, squares2.sem, squares2.at(l, t + 1))
                    inverse_root(l * 4 * TT + 3 * TT + t + 1, 3, t, root_mixed.sem)
                    wait(pool, h2_scaled.sem, h2_scaled.at(l, t + 1))
                    if t == 0:
                        wait(pool, mod2_in.sem, mod2_in.at(l, 64))
                    pool.tensor_tensor(h2[:, t, :], h2[:, t, :], rows[:, 2, t // TL, :], ALU.add).then_inc(h2_ready.sem, 1)
                    wait(pool, h2_ready.sem, h2_ready.at(l, t + 1))
                    pool.dma_start(h_d[t * P:(t + 1) * P, :], h2[:, t, :]).then_inc(h2_out.sem, 16)
                wait(pool, x_mixed.sem, x_mixed.at(l, TT))
                for c in range(2):
                    pool.dma_start(rows[:, 0, c, :], mod_d[c:c + 1, 5 * D:6 * D].broadcast_to((P, D)))\
                        .then_inc(gate2_in.sem, 16)
                wait(pool, routed.sem, routed.at(l, 1))
                wait(pool, list_zeroed, l * 16 + 32)
                for a in range(2):
                    for t in range(TT):
                        pool.indirect_dma_start(
                            out=list_d, out_offset=bass.IndirectOffsetOnAxis(ap=pos_i[:, a * TT + t:a * TT + t + 1], axis=0),
                            in_=tok_i[:, a, t, :], in_offset=None).then_inc(scattered.sem, 16)
                wait(pool, scattered.sem, scattered.at(l, 16 * 2 * TT))
                wait(pool, h2_out.sem, h2_out.at(l, 16 * TT))

                def rounds():
                    n_rounds = pool.value_load(rounds_i[0:1, 0:1], min_val=1, max_val=5)
                    with pool.Fori(0, n_rounds) as r:
                        base = pool.snap(done, min_val=0, max_val=160)
                        wait(pool, hs_in[1], base * 8)
                        wait(pool, place_ready, base)
                        pool.dma_start(list_i[:, :, :].rearrange("p e a -> p (e a)"),
                                       list_d.rearrange("(k e) a -> k (e a)", e=NE)[bass.ds(r * P, P), :])\
                            .then_inc(list_in, 16)
                        wait(pool, list_in, base + 16)

                        def gather(e, b):
                            wait(pool, hs_in[b], base * 8 + (e - b) * 8)
                            pool.tensor_copy(idx_i[:, b:b + 1], list_i[:, bass.ds(e, 1), 0]).then_inc(idx_ready, 1)
                            wait(pool, idx_ready, base + e + 1)
                            wait(pool, hsT_full, base + e + 1)
                            pool.indirect_dma_start(
                                out=hs[:, b, :], out_offset=None, in_=h_d,
                                in_offset=bass.IndirectOffsetOnAxis(ap=idx_i[:, b:b + 1], axis=0)).then_inc(hs_in[b], 16)

                        def scatter(e, b):
                            wait(pool, ys_out[b], base * 8 + (e - b) * 8)
                            pool.tensor_copy(out_i[:, b:b + 1], list_i[:, bass.ds(e, 1), 1]).then_inc(place_ready, 1)
                            wait(pool, place_ready, base + e + 1)
                            wait(pool, ys_low, base + e + 1 + CREDIT)
                            wait(pool, ys_high, base + e + 1 + CREDIT)
                            pool.indirect_dma_start(
                                out=y_d, out_offset=bass.IndirectOffsetOnAxis(ap=out_i[:, b:b + 1], axis=0),
                                in_=ys[:, b, :], in_offset=None).then_inc(ys_out[b], 16)

                        for e in range(3):
                            gather(e, e % 2)
                        with pool.Fori(0, NE // 2 - 2) as i:
                            gather(2 * i + 3, 1)
                            scatter(2 * i, 0)
                            gather(2 * i + 4, 0)
                            scatter(2 * i + 1, 1)
                        gather(NE - 1, 1)
                        for e in range(NE - 4, NE):
                            scatter(e, e % 2)
                        pool.reg_add(done, done, NE)
                rounds()
                empty_lists()
                last = pool.snap(done, min_val=16, max_val=160)
                wait(pool, hsT_full, last + CREDIT)
                wait(pool, ys_out[0], last * 8)
                wait(pool, ys_out[1], last * 8)
                for t in range(TT):
                    b = t % 2
                    wait(pool, x_done.sem, x_done.at(l, max(0, t - 1)))
                    pool.dma_start(hs[:, b, :], y_by[t, 0]).then_inc(yg_in[b].sem, 16)
                    pool.dma_start(ys[:, b, :], y_by[t, 1]).then_inc(yg_in[b].sem, 16)

            for t in range(TT):
                pool.wait_ge(final_squares, t + 1)
                inverse_root(DEPTH * 4 * TT + t + 1, 4, t, final_root)
            pool.wait_ge(list_zeroed, 32 + 16 * DEPTH)

        @block.tensor
        def _(pe):
            mm, tr = pe.matmul, pe.transpose
            for s in (hsT_full, up_full, dn_full):
                pe.sem_inc(s, CREDIT)
            pe.sem_inc(ys_low, CREDIT)
            pe.sem_inc(ys_high, CREDIT)
            pe.wait_ge(const_in, 16 * 11)
            pe.wait_ge(router_in, 16)
            pe.wait_ge(cond_ready, 1)
            done = pe.alloc_register("experts_done_pe")
            pe.reg_mov(done, 0)

            def both(out, lhsT, rhs_of, k, n):
                mm(out[:, 0:N_LAT], lhsT, rhs_of[:, 0:N_LAT], start=(k == 0), stop=(k == n - 1))
                return mm(out[:, N_LAT:N_TOK], lhsT, rhs_of[:, N_LAT:N_TOK], start=(k == 0), stop=(k == n - 1))

            with pe.Fori(0, DEPTH) as l:
                for g in range(3):
                    out = acquire(pe, l, ("ada", g))
                    for k in range(KD):
                        w = view(chunk_wait(pe, l, ("ada", g, k)), 4, 512)
                        for j in range(4):
                            ins = mm(out[32 * j:32 * j + 32, 0:512], cond[:, k, :], w[:, j, :],
                                     start=(k == 0), stop=(k == KD - 1), skip_group_check=True)
                        if k < KD - 1:
                            ins.then_inc(chunk_used.sem, 1)
                    ins.then_inc(psum_full.sem, 1)
                    if g == 0:
                        copied(pe, l, ("ada", 0))
                        out = acquire(pe, l, "modT")
                        for i in range(4):
                            ins = tr(out[:, i * P:(i + 1) * P], mods[:, 0, i * P:(i + 1) * P], ident)
                        ins.then_inc(psum_full.sem, 1)
                for k in range(KD):
                    out = acquire(pe, l, ("h1T", k))
                    for t in range(TT):
                        pe.wait_ge(xn_ready.sem, xn_ready.at(l, t + 1)) if k == 0 else None
                        ins = tr(out[:, t * P:(t + 1) * P], xn[:, t, k * P:(k + 1) * P], ident)
                    ins.then_inc(psum_full.sem, 1)
                copied(pe, l, *[("h1T", k) for k in range(KD)])
                for m in range(10):
                    w = view(chunk_wait(pe, l, ("wT", m // 2)), 2, KD, P)
                    out = acquire(pe, l, ("pT", m))
                    for k in range(KD):
                        ins = both(out, w[:, m % 2, k, :], hT[:, k, :], k, KD)
                    ins.then_inc(psum_full.sem, 1)
                w = [view(chunk_wait(pe, l, ("wN", c)), 2, 928) for c in range(4)]
                for t in range(TT):
                    out = acquire(pe, l, ("pN", t))
                    for k in range(KD):
                        hk = hT[:, k, t * P:(t + 1) * P]
                        mm(out[:, 0:416], hk, w[k // 2][:, k % 2, 0:416], start=(k == 0), stop=(k == KD - 1))
                        ins = mm(out[:, 512:1024], hk, w[k // 2][:, k % 2, 416:928], start=(k == 0), stop=(k == KD - 1))
                    ins.then_inc(psum_full.sem, 1)
                pe.wait_ge(small_in.sem, small_in.at(l, small_in.per_layer))
                for cs in range(2):
                    out = acquire(pe, l, ("fnw", cs))
                    for kk in range(2):
                        ins = mm(out[:, kk * 256:(kk + 1) * 256], chan[:, cs, :], w_fn[:, kk, :],
                                 start=True, stop=True, skip_group_check=True)
                    ins.then_inc(psum_full.sem, 1)
                pe.wait_ge(dft_in.sem, dft_in.at(l, 32))
                copied(pe, l, *[("pN", t) for t in range(TT)])
                for ch in range(2):
                    for cs in range(2):
                        out = acquire(pe, l, ("fnA", ch, cs))
                        lo = 256 + ch * P
                        for t in range(TL):
                            mm(out[:, 0:N_LAT], nat[:, t, lo:lo + P], dft[:, cs, t, :], start=(t == 0), stop=(t == TL - 1))
                        mm(out[:, N_LAT:N_TOK], nat[:, TL, lo:lo + P], dft_c[:, cs, :], start=True, stop=True)\
                            .then_inc(psum_full.sem, 1)
                for kk in range(2):
                    out = acquire(pe, l, ("cqT", kk))
                    for t in range(TT):
                        ins = tr(out[:, t * P:(t + 1) * P], nat[:, t, kk * P:(kk + 1) * P], ident)
                    ins.then_inc(psum_full.sem, 1)
                out = acquire(pe, l, "ckT")
                pe.wait_ge(ckv_ready.sem, ckv_ready.at(l, TT))
                for t in range(TT):
                    ins = tr(out[:, t * P:(t + 1) * P], ckv_n[:, t, :], ident)
                ins.then_inc(psum_full.sem, 1)
                out = acquire(pe, l, "krT")
                pe.wait_ge(kr_ready.sem, kr_ready.at(l, 1))
                for t in range(TT):
                    ins = tr(out[0:ROPE, t * P:(t + 1) * P], kr[:, t, :], ident)
                ins.then_inc(psum_full.sem, 1)
                copied(pe, l, "ckT", ("fnw", 0), ("fnw", 1), *[("fnA", ch, cs) for ch in range(2) for cs in range(2)])
                for p in range(2):
                    out = acquire(pe, l, ("kup", p))
                    w = wkv_up[:, p * P:(p + 1) * P]
                    mm(out[:, 0:512], w, ckvT[:, 0:512], start=True, stop=True)
                    mm(out[:, 512:768], w, ckvT[:, 512:768], start=True, stop=True).then_inc(psum_full.sem, 1)
                for o in range(2):
                    out = acquire(pe, l, ("fnY", o))
                    for n in range(4):
                        ins = both(out, wf[:, n // 2, n % 2, o * P:(o + 1) * P], dftT[:, n // 2, n % 2, :], n, 4)
                    ins.then_inc(psum_full.sem, 1)
                for j in range(3):
                    out = acquire(pe, l, ("vup", j))
                    for n in range(2):
                        c = 2 * j + n
                        ins = mm(out[:, n * 256:(n + 1) * 256], ckvT[:, c * P:(c + 1) * P], wkv_up[:, 256:512],
                                 start=True, stop=True, skip_group_check=True)
                    ins.then_inc(psum_full.sem, 1)
                copied(pe, l, ("cqT", 0), ("cqT", 1))
                for t in range(TT + 1):
                    if t < TT:
                        out = acquire(pe, l, ("qup", t))
                        for kk in range(2):
                            ins = mm(out[:, 0:384], cqT[:, kk, t * P:(t + 1) * P], wq_up[:, kk, :],
                                     start=(kk == 0), stop=(kk == 1))
                        ins.then_inc(psum_full.sem, 1)
                    if t:
                        out = acquire(pe, l, ("qT", t - 1))
                        pe.wait_ge(q_up_ready.sem, q_up_ready.at(l, t))
                        for h in range(HEADS):
                            ins = tr(out[0:QK, h * P:(h + 1) * P], q_up[:, (t - 1) % 2, h * QK:(h + 1) * QK], ident)
                        ins.then_inc(psum_full.sem, 1)
                pe.wait_ge(kv_cache_in.sem, kv_cache_in.at(l, 32))
                pe.wait_ge(v_shifted.sem, v_shifted.at(l, 32))
                pe.wait_ge(krope_in.sem, krope_in.at(l, 16 * HEADS))
                copied(pe, l, *[("pT", m) for m in range(6, 10)], "krT", *[("kup", p) for p in range(2)],
                       *[("qT", t) for t in range(TT)], *[("vup", j) for j in range(3)])
                for step in range(len(UNITS) + 3):
                    for what, u in steps_at(step):
                        kind, h, t = UNITS[u]
                        p = h // 2
                        cols = slice(t * P, (t + 1) * P)
                        if what == "S":
                            out = acquire(pe, l, ("S", u))
                            if kind == "na":
                                mm(out[:, 0:256], q_n[:, h, cols], k_n[:, p, WIN[t]:WIN[t] + 256], start=True, stop=True,
                                   skip_group_check=True)
                                ins = mm(out[:, 256:384], q_n[:, h, cols], k_n[:, p, 512:640], start=True, stop=True,
                                         skip_group_check=True)
                            elif kind == "nac":
                                ins = mm(out[:, 0:P], q_n[:, h, cols], k_n[:, p, 640:768], start=True, stop=True)
                            elif kind == "mlc":
                                ins = mm(out[:, 0:P], q_m[0:QK, h, cols], k_m[0:QK, h, 640:768], start=True, stop=True)
                            else:
                                mm(out[:, 0:512], q_m[0:QK, h, cols], k_m[0:QK, h, 0:512], start=True, stop=True)
                                ins = mm(out[:, 512:640], q_m[0:QK, h, cols], k_m[0:QK, h, 512:640], start=True, stop=True)
                            ins.then_inc(psum_full.sem, 1)
                        elif what == "T":
                            out = acquire(pe, l, ("T", u))
                            pe.wait_ge(probs_ready.sem, probs_ready.at(l, u + 1))
                            for c in range(WIDTH[kind] // P):
                                ins = tr(out[:, c * P:(c + 1) * P], probs[:, u % 3, c * P:(c + 1) * P], ident)
                            ins.then_inc(psum_full.sem, 1)
                        else:
                            key = output_after(u)
                            copied(pe, l, ("T", u - 1), ("T", u))
                            out = acquire(pe, l, key)
                            if kind == "ml":
                                steps = [(probsT[:, hh % 2, c, :], v_m[:, (0, 1, 2, 3, 4)[c], :], c) for c in range(5) for hh in (h - 1, h)]
                                n, width = 5, N_LAT
                            elif kind == "na":
                                vs = (*WIN_V[t], 5)
                                steps = [(probsT_s[:, (u - 1 + i) % 4, c, :], v_n[:, vs[c], :], c) for c in range(3) for i in range(2)]
                                n, width = 3, P
                            else:
                                v = v_n[:, 4, :] if kind == "nac" else v_m[:, 5, :]
                                steps = [(probsT_s[:, (u - 1 + i) % 4, 0, :], v, 0) for i in range(2)]
                                n, width = 1, P
                            for i, (pt, v, c) in enumerate(steps):
                                hh = 2 * p + i % 2
                                lo = 64 * (i % 2)
                                ins = mm(out[lo:lo + 64, 0:width], by_head(v, hh), pt, start=(c == 0), stop=(c == n - 1),
                                         skip_group_check=True)
                            ins.then_inc(psum_full.sem, 1)
                copied(pe, l, ("pT", 2), ("pT", 5), ("fnY", 0), ("fnY", 1),
                       *[output_after(u) for u in range(len(UNITS)) if output_after(u)])
                w = [view(chunk_wait(pe, l, ("wO", c)), 2, D) for c in range(4)]
                for t in range(TT):
                    out = acquire(pe, l, ("out", t))
                    for k in range(KD):
                        for n in range(2):
                            ins = mm(out[:, n * 512:(n + 1) * 512], yT[:, k, t * P:(t + 1) * P],
                                     w[k // 2][:, k % 2, n * 512:(n + 1) * 512], start=(k == 0), stop=(k == KD - 1))
                    ins.then_inc(psum_full.sem, 1)
                for k in range(KD):
                    out = acquire(pe, l, ("h2T", k))
                    for t in range(TT):
                        pe.wait_ge(h2_ready.sem, h2_ready.at(l, t + 1)) if k == 0 else None
                        ins = tr(out[:, t * P:(t + 1) * P], h2[:, t, k * P:(k + 1) * P], ident)
                    ins.then_inc(psum_full.sem, 1)
                copied(pe, l, *[("h2T", k) for k in range(KD)])
                out = acquire(pe, l, "rl")
                for k in range(KD):
                    j = k % 4
                    mm(out[32 * j:32 * j + 32, 0:N_LAT], w_r[:, k, :], h2T[:, k, 0:N_LAT], start=(k < 4), stop=(k >= 4),
                       skip_group_check=True)
                for k in range(KD):
                    j = k % 4
                    ins = mm(out[32 * j:32 * j + 32, N_LAT:N_TOK], w_r[:, k, :], h2T[:, k, N_LAT:N_TOK], start=(k < 4), stop=(k >= 4),
                             skip_group_check=True)
                ins.then_inc(psum_full.sem, 1)
                copied(pe, l, "rl")
                out = acquire(pe, l, "rT")
                for t in range(TT):
                    ins = tr(out[:, t * P:(t + 1) * P], r_log[:, t * P:(t + 1) * P], ident)
                ins.then_inc(psum_full.sem, 1)
                out = acquire(pe, l, "rank")
                pe.wait_ge(mask_ready.sem, mask_ready.at(l, 1))
                m80 = r_mask.rearrange("p a b -> p (a b)")
                mm(out[:, 0:80], before, m80, start=True, stop=True, skip_group_check=True)
                mm(out[:, 128:208], ones, m80, start=True, stop=True, skip_group_check=True).then_inc(psum_full.sem, 1)
                for b in range(8):
                    pe.wait_ge(psum_copied[b].sem, psum_copied[b].at(l, plan.freed[b]))

                def expert_in(base, e, b):
                    pe.wait_ge(hs_in[b], base * 8 + (e - b) * 8 + 16)
                    pe.wait_ge(hsT_ready, base * 2 + e * 2)
                    for k in range(KD):
                        ins = tr(ps[:, k * P:(k + 1) * P], hs[:, b, k * P:(k + 1) * P], ident)
                    ins.then_inc(hsT_full, 1)
                    pe.wait_ge(x13_in[b], base * 16 + (e - b) * 16 + 32)
                    pe.wait_ge(hsT_ready, base * 2 + e * 2 + 2)
                    w = view(at_ring + X13[b] * SLOT, KD, 2 * FF)
                    out = ps[:, (2 + b) * BANK:(3 + b) * BANK]
                    for k in range(KD):
                        ins = mm(out, hsT[b][:, k, :], w[:, k, :], start=(k == 0), stop=(k == KD - 1))
                    ins.then_inc(up_full, 1)

                def expert_out(base, e, b):
                    pe.wait_ge(hid_ready, base + e + 1)
                    for f in range(2):
                        ins = tr(ps[:, (2 + b) * BANK + f * P:(2 + b) * BANK + (f + 1) * P], hid[:, b, f * P:(f + 1) * P], ident)
                    ins.then_inc(hidT_full, 1)
                    pe.wait_ge(x2_in[b], base * 8 + (e - b) * 8 + 16)
                    pe.wait_ge(hidT_ready, base + e + 1)
                    pe.wait_ge(ys_low, base + e + 1)
                    pe.wait_ge(ys_high, base + e + 1)
                    w = ring(X2[b], 2, D)
                    out = ps[:, (4 + 2 * b) * BANK:(6 + 2 * b) * BANK]
                    for n in range(2):
                        for f in range(2):
                            ins = mm(out[:, n * 512:(n + 1) * 512], hidT[:, f, :], w[:, f, n * 512:(n + 1) * 512],
                                     start=(f == 0), stop=(f == 1))
                    ins.then_inc(dn_full, 1)

                def rounds():
                    pe.wait_ge(routed.sem, routed.at(l, 1))
                    pe.sem_inc(passed, 1)
                    n_rounds = pe.value_load(rounds_i[0:1, 0:1], min_val=1, max_val=5)
                    with pe.Fori(0, n_rounds):
                        base = pe.snap(done, min_val=0, max_val=160)
                        expert_in(base, 0, 0)
                        with pe.Fori(0, NE // 2 - 1) as i:
                            expert_in(base, 2 * i + 1, 1)
                            expert_out(base, 2 * i, 0)
                            expert_in(base, 2 * i + 2, 0)
                            expert_out(base, 2 * i + 1, 1)
                        expert_in(base, NE - 1, 1)
                        expert_out(base, NE - 2, 0)
                        expert_out(base, NE - 1, 1)
                        pe.reg_add(done, done, NE)
                rounds()

        @block.scalar
        def _(act):
            act.wait_ge(x_in, 16 * (TT + 1))
            act.activation(c_exp, c_raw, ACT.Exp, scale=-1.0).then_inc(cond_exp, 1)
            done = act.alloc_register("experts_done_act")
            act.reg_mov(done, 0)
            with act.Fori(0, DEPTH) as l:
                act.wait_ge(x_done.sem, x_done.at(l, 0))
                for t in range(TT):
                    act.wait_ge(squares.sem, squares.at(l, t))
                    act.activation(junk, x[:, t, :], ACT.Square, scale=D ** -0.5,
                                   accum_out=stat[:, 0, t:t + 1]).then_inc(squares.sem, 1)
                copied(act, l, "modT")
                for k in range(KD):
                    out = filled(act, l, ("h1T", k))
                    act.activation(hT[:, k, N_LAT:N_TOK], out[:, N_LAT:N_TOK], ACT.Identity,
                                   scale=mod_a[:, 1, k:k + 1], bias=mod_s[:, 1, k:k + 1]).then_inc(bank_of(("h1T", k)), 1)
                act.wait_ge(bias_ready.sem, bias_ready.at(l, 1))
                for c in range(2):
                    out = filled(act, l, ("pT", 3 * c))
                    if c == 1:
                        copied(act, l, ("pT", 1))
                    act.activation(c_sb, out[:, 0:N_TOK], ACT.Copy).then_inc(bank_of(("pT", 3 * c)), 1)
                act.wait_ge(q_zeroed.sem, q_zeroed.at(l, 1))
                for p in range(2):
                    out = filled(act, l, ("pT", 6 + p))
                    act.activation(q_n[0:64, 2 * p, :], out[0:64, 0:N_TOK], ACT.Copy)
                    act.activation(q_n[64:128, 2 * p + 1, :], out[64:128, 0:N_TOK], ACT.Copy).then_inc(bank_of(("pT", 6 + p)), 1)
                copied(act, l, ("pT", 2), ("pT", 5))
                for t in range(TT):
                    out = filled(act, l, ("pN", t))
                    act.wait_ge(kv_squares.sem, kv_squares.at(l, 2 * t))
                    act.activation(sq_junk, out[:, 512:768], ACT.Square, scale=256 ** -0.5,
                                   accum_out=stat[:, 1, t:t + 1]).then_inc(kv_squares.sem, 1)
                    act.activation(nat[:, t, :], out[:, 512:1024], ACT.Copy).then_inc(bank_of(("pN", t)), 1)
                    act.wait_ge(ckv_raw.sem, ckv_raw.at(l, t + 1))
                    act.wait_ge(kv_squares.sem, kv_squares.at(l, 2 * t + 1))
                    act.activation(sq_junk[:, 0:P], ckv_n[:, t, :], ACT.Square, scale=P ** -0.5,
                                   accum_out=stat[:, 2, t:t + 1]).then_inc(kv_squares.sem, 1)
                act.wait_ge(small_in.sem, small_in.at(l, small_in.per_layer))
                for cs in range(2):
                    out = filled(act, l, ("fnw", cs))
                    act.activation(wf[:, cs, :, :], out[:, 0:512].rearrange("p (a b) -> p a b", a=2), ACT.Copy)\
                        .then_inc(bank_of(("fnw", cs)), 1)
                for ch in range(2):
                    out = filled(act, l, ("fnA", ch, 1))
                    act.activation(dftT[:, 1, ch, :], out[:, 0:N_TOK], ACT.Copy).then_inc(bank_of(("fnA", ch, 1)), 1)
                for kk in range(2):
                    out = filled(act, l, ("cqT", kk))
                    act.activation(cqT[:, kk, :], out[:, 0:N_TOK], ACT.Copy, scale=gq[:, kk:kk + 1])\
                        .then_inc(bank_of(("cqT", kk)), 1)
                out = filled(act, l, "krT")
                for h in range(HEADS):
                    ins = act.activation(k_m[64:96, h, 0:N_LAT], out[0:ROPE, 0:N_LAT], ACT.Copy)
                ins.then_inc(bank_of("krT"), 1)
                for p in range(2):
                    out = filled(act, l, ("kup", p))
                    act.activation(k_m[0:64, 2 * p, :], out[0:64, 0:768], ACT.Copy)
                    act.activation(k_m[0:64, 2 * p + 1, :], out[64:128, 0:768], ACT.Copy).then_inc(bank_of(("kup", p)), 1)
                for j in range(3):
                    out = filled(act, l, ("vup", j))
                    act.activation(v_m[:, 2 * j:2 * j + 2, :], out[:, 0:512].rearrange("p (a b) -> p a b", a=2), ACT.Copy)\
                        .then_inc(bank_of(("vup", j)), 1)
                for t in range(TT):
                    out = filled(act, l, ("qup", t))
                    act.wait_ge(root_q.sem, root_q.at(l, t + 1))
                    act.activation(q_up[:, t % 2, :], out[:, 0:384], ACT.Copy, scale=rstd[:, 1, t:t + 1])\
                        .then_inc(bank_of(("qup", t)), 1)
                for step in range(len(UNITS) + 2):
                    if step < len(UNITS):
                        u = step
                        kind, h, t = UNITS[u]
                        out = filled(act, l, ("S", u))
                        pr = probs[:, u % 3, 0:WIDTH[kind]]
                        if kind == "na":
                            act.wait_ge(max_ready.sem, max_ready.at(l, u + 1))
                            act.activation(pr, pr, ACT.Exp, bias=negmax[:, u % 4:u % 4 + 1],
                                           accum_out=rowsum[:, u % 4:u % 4 + 1]).then_inc(exp_ready.sem, 1)
                        else:
                            act.wait_ge(max_ready.sem, max_ready.at(l, u + 1))
                            act.activation(pr, out[:, 0:WIDTH[kind]], ACT.Exp, bias=negmax[:, u % 4:u % 4 + 1],
                                           scale=(HD if kind == "nac" else QK) ** -0.5,
                                           accum_out=rowsum[:, u % 4:u % 4 + 1]).then_inc(bank_of(("S", u)), 1)
                    if step >= 2:
                        u = step - 2
                        kind, h, t = UNITS[u]
                        last = {24: ("mlcO", 1, TL), 32: ("mlO", 0, 0)}.get(u, ("T", u))
                        filled(act, l, last)
                        out = place(("T", u))
                        wd = WIDTH[kind]
                        src = out[:, 0:wd].rearrange("p (a b) -> p a b", a=wd // P)
                        if kind == "ml":
                            dst = probsT[:, h % 2, :, t * P:(t + 1) * P]
                        else:
                            dst = probsT_s[:, u % 4, 0:wd // P, :]
                        act.activation(dst, src, ACT.Copy).then_inc(bank_of(("T", u)), 1)
                for t in range(TT):
                    act.wait_ge(x_mixed.sem, x_mixed.at(l, t + 1))
                    act.wait_ge(squares2.sem, squares2.at(l, t))
                    act.activation(junk, x[:, t, :], ACT.Square, scale=D ** -0.5,
                                   accum_out=stat[:, 3, t:t + 1]).then_inc(squares2.sem, 1)
                for k in range(KD):
                    out = filled(act, l, ("h2T", k))
                    act.activation(h2T[:, k, N_LAT:N_TOK], out[:, N_LAT:N_TOK], ACT.Copy).then_inc(bank_of(("h2T", k)), 1)
                act.wait_ge(logits_ready.sem, logits_ready.at(l, 1))
                act.activation(r_s, r_z, ACT.Exp, scale=-1.0).then_inc(rexp_ready.sem, 1)

                def tokens(base, e, b):
                    act.wait_ge(hsT_full, base + e + 1 + CREDIT)
                    act.wait_ge(up_full, base + e - 1 + CREDIT)
                    act.activation(hsT[b][:, 4:8, :], ps[:, 512:1024].rearrange("p (a b) -> p a b", a=4), ACT.Copy)\
                        .then_inc(hsT_ready, 1)

                def back(base, e):
                    b = e % 2
                    act.wait_ge(hidT_full, base + e + 1)

                def hidden_back(base, e, b):
                    act.wait_ge(hidT_full, base + e + 1)
                    act.wait_ge(dn_full, base + e + CREDIT)
                    act.activation(hidT, ps[:, (2 + b) * BANK:(2 + b) * BANK + FF].rearrange("p (a b) -> p a b", a=2),
                                   ACT.Copy).then_inc(hidT_ready, 1)

                def hidden(base, e, b):
                    act.wait_ge(up_full, base + e + 1 + CREDIT)
                    act.wait_ge(hid_ready, base + e)
                    act.activation(ff_t[:, b, :], ps[:, (2 + b) * BANK:(2 + b) * BANK + FF], ACT.Exp, scale=-1.0)\
                        .then_inc(e_ready, 1)

                def output(base, e, b):
                    act.wait_ge(dn_full, base + e + 1 + CREDIT)
                    act.wait_ge(ys_out[b], base * 8 + (e - b) * 8)
                    lo = (4 + 2 * b) * BANK
                    act.activation(ys[:, b, 512:1024], ps[:, lo + 512:lo + 1024], ACT.Copy).then_inc(ys_high, 1)

                def rounds():
                    act.wait_ge(routed.sem, routed.at(l, 1))
                    act.sem_inc(passed, 1)
                    n_rounds = act.value_load(rounds_i[0:1, 0:1], min_val=1, max_val=5)
                    with act.Fori(0, n_rounds):
                        base = act.snap(done, min_val=0, max_val=160)

                        def step(e_in, b):
                            tokens(base, e_in, b)
                            hidden_back(base, e_in - 1, 1 - b)
                            hidden(base, e_in, b)
                            output(base, e_in - 1, 1 - b)

                        tokens(base, 0, 0)
                        hidden(base, 0, 0)
                        with act.Fori(0, NE // 2 - 1) as i:
                            step(2 * i + 1, 1)
                            step(2 * i + 2, 0)
                        step(NE - 1, 1)
                        hidden_back(base, NE - 1, 1)
                        output(base, NE - 1, 1)
                        act.reg_add(done, done, NE)
                rounds()
                for t in range(TT):
                    b = t % 2
                    act.wait_ge(yg_in[b].sem, yg_in[b].at(l, 32 * (t // 2 + 1)))
                    act.activation(hs[:, b, :], hs[:, b, :], ACT.Copy, scale=gates[:, 0, t:t + 1]).then_inc(y_first.sem, 1)
            for t in range(TT):
                act.wait_ge(x_done.sem, x_done.at(DEPTH - 1, t + 1))
                if t:
                    act.wait_ge(final_squares, t)
                act.activation(junk, x[:, t, :], ACT.Square, scale=D ** -0.5,
                               accum_out=stat[:, 4, t:t + 1]).then_inc(final_squares, 1)
            for t in range(TT):
                act.wait_ge(y_final, t + 1)
                act.dma_start(O["y"][t * P:(t + 1) * P, :], h2[:, t, :]).then_inc(y_out, 16)

        @block.vector
        def _(dve):
            V = dve.tensor_tensor
            dve.wait_ge(cond_exp, 1)
            dve.tensor_scalar(c_exp, c_exp, 1.0, None, ALU.add).then_inc(cond_step, 1)
            dve.wait_ge(cond_step, 1)
            dve.reciprocal(c_exp, c_exp).then_inc(cond_step, 1)
            dve.wait_ge(cond_step, 2)
            V(c_raw, c_raw, c_exp, ALU.mult).then_inc(cond_step, 1)
            dve.wait_ge(cond_step, 3)
            dve.tensor_copy(cond.rearrange("p k (c n) -> p k c n", c=2),
                            c_raw.unsqueeze(3).broadcast_to((P, KD, 2, 16))).then_inc(cond_ready, 1)
            dve.wait_ge(const_in, 16 * 11)
            done = dve.alloc_register("experts_done_dve")
            dve.reg_mov(done, 0)
            links = [0]
            with dve.Fori(0, DEPTH) as l:

                def link(ins):
                    links[0] += 1
                    ins.then_inc(dve_chain.sem, 1)
                    dve.wait_ge(dve_chain.sem, dve_chain.at(l, links[0]))

                dve.wait_ge(x_in, 16 * (TT + 1))
                for t in range(TT):
                    dve.wait_ge(root_x.sem, root_x.at(l, t + 1))
                    dve.tensor_scalar(xn[:, t, :], x[:, t, :], rstd[:, 0, t:t + 1], None, ALU.mult).then_inc(xn_ready.sem, 1)
                dve.wait_ge(ada_in.sem, ada_in.at(l, ada_in.per_layer))
                for g in range(3):
                    out = filled(dve, l, ("ada", g))
                    V(mods[:, g, :], out[:, 0:512], b_ada[:, g, :], ALU.add).then_inc(bank_of(("ada", g)), 1)
                    if g == 0:
                        out = filled(dve, l, "modT").rearrange("p (i q) -> p i q", i=4)
                        for c in range(2):
                            for v in range(2):
                                src = out[:, :, 64 * v + 16 * c:64 * v + 16 * c + 33:32].rearrange("p i j -> p j i")
                                dst = (mod_s, mod_a)[v][:, c, :].rearrange("p (j i) -> p j i", j=2)
                                if v:
                                    ins = dve.scalar_tensor_tensor(out=dst, in0=src, scalar=1.0,
                                                                   in1=n1c.rearrange("p (j i) -> p j i", j=2),
                                                                   op0=ALU.add, op1=ALU.mult)
                                else:
                                    ins = dve.tensor_copy(dst, src)
                        ins.then_inc(bank_of("modT"), 1)
                        copied(dve, l, "modT")
                        for k in range(KD):
                            out = filled(dve, l, ("h1T", k)) if False else None
                copied(dve, l, ("ada", 2))
                dve.scalar_tensor_tensor(out=mods[0:64, 2, :], in0=mods[0:64, 2, :], scalar=1.0, in1=n2q[0:64, :],
                                         op0=ALU.add, op1=ALU.mult).then_inc(mods_scaled.sem, 1)
                for k in range(KD):
                    out = filled(dve, l, ("h1T", k))
                    dve.tensor_scalar(hT[:, k, 0:N_LAT], out[:, 0:N_LAT], mod_a[:, 0, k:k + 1], mod_s[:, 0, k:k + 1],
                                      ALU.mult, ALU.add).then_inc(bank_of(("h1T", k)), 1)
                dve.wait_ge(bias_ready.sem, bias_ready.at(l, 1))
                for zero in (z_lat[:, 0:1], z_lat[:, 527:528], z_ctx[:, 0:1]):
                    dve.memset(zero, 0.0)
                link(dve.memset(z_ctx[:, 129:130], 0.0))
                for c in range(2):
                    out = filled(dve, l, ("pT", 3 * c + 1))
                    copied(dve, l, ("pT", 3 * c))
                    V(z_lat[:, 8:520], out[:, 0:N_LAT], c_sb[:, 0:N_LAT], ALU.mult)
                    V(z_ctx[:, 1:129], out[:, N_LAT:N_TOK], c_sb[:, N_LAT:N_TOK], ALU.mult).then_inc(bank_of(("pT", 3 * c + 1)), 1)
                    copied(dve, l, ("pT", 3 * c + 1))
                    dve.tensor_copy(z_lat[:, 1:8], z_lat[:, 512:519])
                    link(dve.tensor_copy(z_lat[:, 520:527], z_lat[:, 9:16]))
                    w = [convw[:, c, i:i + 1] for i in range(3)]
                    parts = [(cv[:, 0:N_LAT], z_lat, 8, N_LAT), (cv[:, N_LAT:N_TOK], z_ctx, 1, N_CTX)]
                    for i, n in enumerate((1, 0, 2)):
                        for dst, z, s, m in parts:
                            if i == 0:
                                ins = dve.tensor_scalar(dst, z[:, s:s + m], w[1], None, ALU.mult)
                            else:
                                ins = dve.scalar_tensor_tensor(out=dst, in0=z[:, n * s:n * s + m], scalar=w[n], in1=dst,
                                                               op0=ALU.mult, op1=ALU.add)
                        link(ins)
                    out = filled(dve, l, ("pT", 3 * c + 2))
                    V(yT[:, c, :], out[:, 0:N_TOK], cv, ALU.mult).then_inc(bank_of(("pT", 3 * c + 2)), 1)
                dve.wait_ge(q_zeroed.sem, q_zeroed.at(l, 1))
                for p in range(2):
                    out = filled(dve, l, ("pT", 8 + p))
                    dve.tensor_copy(k_n[:, p, 0:N_LAT], out[:, 0:N_LAT])
                    dve.tensor_copy(k_n[:, p, 640:768], out[:, N_LAT:N_TOK]).then_inc(bank_of(("pT", 8 + p)), 1)
                dve.wait_ge(small_in.sem, small_in.at(l, small_in.per_layer))
                for t in range(TT):
                    out = filled(dve, l, ("pN", t))
                    dve.tensor_copy(v_n[:, t, :], out[:, 0:256])
                    dve.tensor_copy(ckv_n[:, t, :], out[:, 256:384]).then_inc(ckv_raw.sem, 1)
                    dve.tensor_copy(kr[:, t, :], out[:, 384:416]).then_inc(bank_of(("pN", t)), 1)
                for t in range(TT):
                    dve.wait_ge(root_kv.sem, root_kv.at(l, t + 1))
                    dve.scalar_tensor_tensor(out=ckv_n[:, t, :], in0=ckv_n[:, t, :], scalar=rstd[:, 2, t:t + 1], in1=gkv,
                                             op0=ALU.mult, op1=ALU.mult).then_inc(ckv_ready.sem, 1)

                def rotate(v, cos, sin, shape):
                    n = int(np.prod(shape))
                    tm = [tmp4[:, i, 0:n].rearrange("p (a b f) -> p a b f", a=shape[0], b=shape[1]) for i in range(4)]
                    x1, x2 = v[:, :, :, 0, :], v[:, :, :, 1, :]
                    V(tm[0], x1, cos, ALU.mult)
                    V(tm[1], x2, sin, ALU.mult)
                    V(tm[2], x1, sin, ALU.mult)
                    link(V(tm[3], x2, cos, ALU.mult))
                    V(x1, tm[0], tm[1], ALU.subtract)
                    return V(x2, tm[3], tm[2], ALU.add)

                copied(dve, l, ("pN", TT - 1))
                r4 = rope.rearrange("p c t (a f) -> p c t a f", a=2)
                rotate(kr[:, 0:TL, :].rearrange("p t (a h f) -> p t a h f", a=2, h=2), r4[:, 0], r4[:, 1], (TL, 2, 8))\
                    .then_inc(kr_ready.sem, 1)
                for ch in range(2):
                    out = filled(dve, l, ("fnA", ch, 0))
                    dve.tensor_copy(dftT[:, 0, ch, :], out[:, 0:N_TOK]).then_inc(bank_of(("fnA", ch, 0)), 1)
                out = filled(dve, l, "ckT")
                dve.tensor_copy(ckvT[:, 0:N_LAT], out[:, 0:N_LAT])
                dve.tensor_copy(ckvT[:, 640:768], out[:, N_LAT:N_TOK]).then_inc(bank_of("ckT"), 1)
                out = filled(dve, l, "krT")
                for h in range(HEADS):
                    ins = dve.tensor_copy(k_m[64:96, h, 640:768], out[0:ROPE, N_LAT:N_TOK])
                ins.then_inc(bank_of("krT"), 1)
                for o in range(2):
                    out = filled(dve, l, ("fnY", o))
                    dve.tensor_copy(yT[:, 6 + o, :], out[:, 0:N_TOK]).then_inc(bank_of(("fnY", o)), 1)
                for t in range(TT):
                    copied(dve, l, ("qup", t))
                    q = q_up[:, t % 2, :].rearrange("p (h n) -> p h n", h=HEADS)[:, :, HD:QK]
                    if t < TL:
                        shape = (P, HEADS, 2, 8)
                        rotate(q.rearrange("p h (a x f) -> p h a x f", a=2, x=2), r4[:, 0, t].unsqueeze(1).broadcast_to(shape),
                               r4[:, 1, t].unsqueeze(1).broadcast_to(shape), (HEADS, 2, 8)).then_inc(q_up_ready.sem, 1)
                    else:
                        dve.tensor_copy(tmp4[:, 0, 0:1], tmp4[:, 1, 0:1]).then_inc(q_up_ready.sem, 1)
                    out = filled(dve, l, ("qT", t))
                    dve.tensor_copy(q_m[0:QK, :, t * P:(t + 1) * P],
                                    out[0:QK, 0:512].rearrange("p (h n) -> p h n", h=HEADS)).then_inc(bank_of(("qT", t)), 1)
                for step in range(len(UNITS) + 3):
                    if step < len(UNITS):
                        u = step
                        kind, h, t = UNITS[u]
                        wd = WIDTH[kind]
                        out = filled(dve, l, ("S", u))
                        col = slice(u % 4, u % 4 + 1)
                        src, factor = out[:, 0:wd], -(QK if kind[0] == "m" else HD) ** -0.5
                        if kind == "na":
                            dve.scalar_tensor_tensor(out=probs[:, u % 3, 0:256], in0=out[:, 0:256], scalar=HD ** -0.5,
                                                     in1=bias[:, h, BIAS_KIND[t], :], op0=ALU.mult, op1=ALU.add)
                            dve.tensor_scalar(probs[:, u % 3, 256:384], out[:, 256:384], HD ** -0.5, None, ALU.mult)\
                                .then_inc(bank_of(("S", u)), 1)
                            copied(dve, l, ("S", u))
                            src, factor = probs[:, u % 3, 0:wd], -1.0
                        link(dve.tensor_reduce(rowmax[:, col], src, AX.X, ALU.max))
                        dve.tensor_scalar(negmax[:, col], rowmax[:, col], factor, None, ALU.mult).then_inc(max_ready.sem, 1)
                        if kind == "na":
                            dve.wait_ge(exp_ready.sem, exp_ready.at(l, u + 1))
                        else:
                            copied(dve, l, ("S", u))
                        dve.reciprocal(rowinv[:, col], rowsum[:, col]).then_inc(inv_ready.sem, 1)
                    if step >= 3 and output_after(step - 3):
                        key = output_after(step - 3)
                        kind, p, t = key
                        out = filled(dve, l, key)
                        k = p + (2 if kind[0] == "n" else 4)
                        dst = yT[:, k, 0:N_LAT] if kind == "mlO" else yT[:, k, t * P:(t + 1) * P]
                        dve.tensor_copy(dst, out[:, 0:N_LAT if kind == "mlO" else P]).then_inc(bank_of(key), 1)
                dve.wait_ge(gate1_in.sem, gate1_in.at(l, 32))
                dve.wait_ge(mod2_in.sem, mod2_in.at(l, 64))
                for step in range(TT + 1):
                    if step < TT:
                        t = step
                        out = filled(dve, l, ("out", t))
                        V(hs[:, t % 2, :], out[:, 0:D], rows[:, 0, t // TL, :], ALU.mult).then_inc(bank_of(("out", t)), 1)
                        copied(dve, l, ("out", t))
                        V(x[:, t, :], x[:, t, :], hs[:, t % 2, :], ALU.add).then_inc(x_mixed.sem, 1)
                    if step:
                        t = step - 1
                        dve.wait_ge(root_mixed.sem, root_mixed.at(l, t + 1))
                        dve.scalar_tensor_tensor(out=h2[:, t, :], in0=x[:, t, :], scalar=rstd[:, 3, t:t + 1],
                                                 in1=rows[:, 1, t // TL, :], op0=ALU.mult, op1=ALU.mult)\
                            .then_inc(h2_scaled.sem, 1)
                for k in range(KD):
                    out = filled(dve, l, ("h2T", k))
                    dve.tensor_copy(h2T[:, k, 0:N_LAT], out[:, 0:N_LAT]).then_inc(bank_of(("h2T", k)), 1)
                out = filled(dve, l, "rl")
                dve.tensor_copy(r_log, out[:, 0:N_TOK]).then_inc(bank_of("rl"), 1)
                out = filled(dve, l, "rT")[:, 0:N_TOK].rearrange("p (t j e) -> p t e j", t=TT, j=4)
                link(dve.tensor_reduce(r_z, out[:, :, 0:NE, :], AX.X, ALU.add))
                dve.tensor_copy(r_z, r_z).then_inc(bank_of("rT"), 1)
                copied(dve, l, "rT")
                dve.tensor_copy(r_t, r_z).then_inc(logits_ready.sem, 1)
                dve.wait_ge(rexp_ready.sem, rexp_ready.at(l, 1))
                link(dve.tensor_scalar(r_s, r_s, 1.0, None, ALU.add))
                link(dve.reciprocal(r_s, r_s))
                link(V(r_sb, r_s, b_r.unsqueeze(1).broadcast_to((P, TT, NE)), ALU.add))
                grp = r_sb.rearrange("p t (g e) -> p (t g) e", g=4)
                V(r_pair[:, :, 0:3], grp[:, :, 0:3], grp[:, :, 1:4], ALU.add)
                V(r_pair[:, :, 3:5], grp[:, :, 0:2], grp[:, :, 2:4], ALU.add)
                link(V(r_pair[:, :, 5:6], grp[:, :, 0:1], grp[:, :, 3:4], ALU.add))

                def first_of_max(dst, val, count, n, tmp, mx):
                    bc = (P, TT, n)
                    link(dve.tensor_reduce(mx, val, AX.X, ALU.max))
                    link(V(tmp, val, mx.unsqueeze(2).broadcast_to(bc), ALU.is_equal))
                    link(V(tmp, tmp, count.unsqueeze(1).broadcast_to(bc), ALU.mult))
                    link(dve.tensor_reduce(mx, tmp, AX.X, ALU.max))
                    link(V(dst, tmp, mx.unsqueeze(2).broadcast_to(bc), ALU.is_equal))

                link(dve.tensor_reduce(r_g.rearrange("p t g -> p (t g)"), r_pair, AX.X, ALU.max))
                first_of_max(r_first, r_g, count4, 4, r_t[:, :, 0:4], r_gm)
                flag = r_first.rearrange("p t g -> p (t g)").unsqueeze(2).broadcast_to((P, 4 * TT, 4))
                V(r_m.rearrange("p t (g e) -> p (t g) e", g=4), grp, flag, ALU.mult)
                link(dve.tensor_scalar(r_t.rearrange("p t (g e) -> p (t g) e", g=4), flag, -MASKED, MASKED, ALU.mult, ALU.add))
                link(V(r_m, r_m, r_t, ALU.add))
                for a in range(2):
                    first_of_max(r_sel[:, a], r_m, count16, NE, r_t, r_gm)
                    if a == 0:
                        link(dve.scalar_tensor_tensor(out=r_m, in0=r_sel[:, 0], scalar=10 * MASKED, in1=r_m,
                                                      op0=ALU.mult, op1=ALU.add))
                V(r_mask, r_sel[:, 0], r_sel[:, 1], ALU.add).then_inc(mask_ready.sem, 1)
                for a in range(2):
                    link(V(r_t, r_sel[:, a], r_s, ALU.mult))
                    link(dve.tensor_reduce(r_w[:, a], r_t, AX.X, ALU.add))
                link(V(r_gm, r_w[:, 0], r_w[:, 1], ALU.add))
                link(dve.reciprocal(r_gm, r_gm))
                V(gates, r_w, r_gm.unsqueeze(1).broadcast_to((P, 2, TT)), ALU.mult)
                out = filled(dve, l, "rank")
                link(dve.memset(r_cum[:, 0, :], 0.0))
                for t in range(TT):
                    link(V(r_cum[:, t + 1, :], out[:, 128 + t * NE:128 + (t + 1) * NE], r_cum[:, t, :], ALU.add))
                V(r_rank, out[:, 0:80].rearrange("p (t e) -> p t e", t=TT), r_cum[:, 0:TT, :], ALU.add).then_inc(bank_of("rank"), 1)
                copied(dve, l, "rank")
                link(dve.scalar_tensor_tensor(out=r_rank, in0=r_rank, scalar=float(NE),
                                              in1=iota16.unsqueeze(1).broadcast_to((P, TT, NE)), op0=ALU.mult, op1=ALU.add))
                for a in range(2):
                    link(V(r_t, r_sel[:, a], r_rank, ALU.mult))
                    link(dve.tensor_reduce(r_pos[:, a], r_t, AX.X, ALU.add))
                dve.tensor_copy(pos_i[:, :], r_pos.rearrange("p a t -> p (a t)"))
                link(dve.tensor_reduce(r_n[:, 0:1], r_cum[:, TT, :], AX.X, ALU.max))
                link(dve.tensor_scalar(r_n[:, 1:5], limits, r_n[:, 0:1], None, ALU.is_lt))
                link(dve.tensor_reduce(r_n[:, 5:6], r_n[:, 1:5], AX.X, ALU.add))
                dve.tensor_scalar(rounds_i[:, 0:1], r_n[:, 5:6], 1.0, None, ALU.add).then_inc(routed.sem, 1)

                def tokens(base, e, b):
                    dve.wait_ge(hsT_full, base + e + 1 + CREDIT)
                    dve.wait_ge(up_full, base + e - 1 + CREDIT)
                    dve.tensor_copy(hsT[b][:, 0:4, :], ps[:, 0:512].rearrange("p (a b) -> p a b", a=4)).then_inc(hsT_ready, 1)

                def hidden(base, e, b):
                    dve.wait_ge(e_ready, base + e + 1)
                    dve.wait_ge(up_full, base + e + 1 + CREDIT)
                    lo = (2 + b) * BANK
                    f = ff_t[:, b, :]
                    dve.tensor_scalar(f, f, 1.0, None, ALU.add).then_inc(silu_chain, 1)
                    dve.wait_ge(silu_chain, (base + e) * 3 + 1)
                    dve.reciprocal(f, f).then_inc(silu_chain, 1)
                    dve.wait_ge(silu_chain, (base + e) * 3 + 2)
                    V(f, ps[:, lo:lo + FF], f, ALU.mult).then_inc(silu_chain, 1)
                    dve.wait_ge(silu_chain, (base + e) * 3 + 3)
                    V(hid[:, b, :], ps[:, lo + FF:lo + 2 * FF], f, ALU.mult).then_inc(hid_ready, 1)

                def output(base, e, b):
                    dve.wait_ge(dn_full, base + e + 1 + CREDIT)
                    dve.wait_ge(ys_out[b], base * 8 + (e - b) * 8)
                    lo = (4 + 2 * b) * BANK
                    dve.tensor_copy(ys[:, b, 0:512], ps[:, lo:lo + 512]).then_inc(ys_low, 1)

                def rounds():
                    n_rounds = dve.value_load(rounds_i[0:1, 0:1], min_val=1, max_val=5)
                    with dve.Fori(0, n_rounds):
                        base = dve.snap(done, min_val=0, max_val=160)

                        def step(e_in, b):
                            tokens(base, e_in, b)
                            hidden(base, e_in, b)
                            output(base, e_in - 1, 1 - b)

                        tokens(base, 0, 0)
                        hidden(base, 0, 0)
                        with dve.Fori(0, NE // 2 - 1) as i:
                            step(2 * i + 1, 1)
                            step(2 * i + 2, 0)
                        step(NE - 1, 1)
                        output(base, NE - 1, 1)
                        dve.reg_add(done, done, NE)
                dve.wait_ge(routed.sem, routed.at(l, 1))
                dve.sem_inc(passed, 1)
                rounds()
                dve.wait_ge(gate2_in.sem, gate2_in.at(l, 32))
                for t in range(TT):
                    b = t % 2
                    dve.wait_ge(yg_in[b].sem, yg_in[b].at(l, 32 * (t // 2 + 1)))
                    dve.wait_ge(y_first.sem, y_first.at(l, t + 1))
                    link(dve.scalar_tensor_tensor(out=ys[:, b, :], in0=ys[:, b, :], scalar=gates[:, 1, t:t + 1],
                                                  in1=hs[:, b, :], op0=ALU.mult, op1=ALU.add))
                    link(V(ys[:, b, :], ys[:, b, :], rows[:, 0, t // TL, :], ALU.mult))
                    V(x[:, t, :], x[:, t, :], ys[:, b, :], ALU.add).then_inc(x_done.sem, 1)
            assert links[0] == DVE_CHAIN, links[0]
            assert copies == plan.copies, {k: (copies.get(k), n) for k, n in plan.copies.items() if copies.get(k) != n}
            dve.wait_ge(normf_in, 16)
            for t in range(TT):
                dve.wait_ge(final_root, t + 1)
                dve.scalar_tensor_tensor(out=h2[:, t, :], in0=x[:, t, :], scalar=rstd[:, 4, t:t + 1], in1=normf_row,
                                         op0=ALU.mult, op1=ALU.mult).then_inc(y_final, 1)


def grid_order():
    return np.arange(N_LAT).reshape(GRID_H, GRID_W).T.ravel()


def shape_constants():
    order = grid_order()
    c = {}
    c["c_ident"] = np.eye(P, dtype=np.float32)
    c["c_before"] = np.triu(np.ones((P, P), np.float32), 1)
    c["c_ones"] = np.ones((P, P), np.float32)
    ang = 2 * np.pi * (np.outer(np.arange(HD), np.arange(HD)) % HD) / HD
    chan = np.zeros((P, 2, P))
    for g in range(2):
        s = slice(g * HD, (g + 1) * HD)
        chan[s, 0, s], chan[s, 1, s] = np.cos(ang), -np.sin(ang)
    c["c_chan"] = chan.astype(np.float32)

    def dft(places, n):
        a = 2 * np.pi * (np.outer(places, places) % n) / n
        return np.stack([np.cos(a), np.sin(a)]) / np.sqrt(n * HD)

    lat = dft(order, N_LAT).reshape(2, TL, P, N_LAT).transpose(2, 0, 1, 3)
    c["c_dft"] = np.ascontiguousarray(lat.reshape(P, -1)).astype(np.float32)
    ctx = dft(np.arange(N_CTX), N_CTX).transpose(1, 0, 2)
    c["c_dft_ctx"] = np.ascontiguousarray(ctx.reshape(P, -1)).astype(np.float32)
    pos = np.stack([order // GRID_W, order % GRID_W], -1).astype(np.float32)
    nf = ROPE // 4
    freqs = np.float32(10000.0) ** (-np.arange(nf, dtype=np.float32) / nf)
    ang = (pos[:, :, None] * freqs).astype(np.float32)
    rope = np.stack([np.cos(ang), np.sin(ang)]).reshape(2, TL, P, 2 * nf).transpose(2, 0, 1, 3)
    c["c_rope"] = np.ascontiguousarray(rope).astype(np.float32)
    c["c_iota"] = np.tile(np.arange(NE, dtype=np.float32), (P, 1))
    c["c_count"] = np.tile(np.arange(NE, 0, -1, dtype=np.float32), (P, 1))
    c["c_limits"] = np.tile(np.arange(1, 5, dtype=np.float32) * P, (P, 1))
    token = np.arange(P)[:, None, None] + P * np.arange(TT)[None, None] + np.zeros((1, 2, 1), np.int64)
    c["c_tok"] = np.stack([token, 2 * token + np.arange(2)[None, :, None]], -1).astype(np.int32)
    masks = np.zeros((P, 3, 256), np.float32)
    for kind, t in enumerate((0, 1, 3)):
        q = (np.arange(P) // GRID_H + 16 * t)[:, None]
        k = (np.arange(256) // GRID_H + WIN[t] // GRID_H)[None]
        start = np.clip(q - NK // 2, 0, GRID_W - NK)
        masks[:, kind] = np.where((k >= start) & (k < start + NK), 0.0, MASKED)
    c["c_masks"] = masks
    return c


def laid_out(inputs):
    a = {k: np.asarray(v) for k, v in inputs.items()}
    order = grid_order()
    o = {}
    o["x_all"] = np.concatenate([a["x_sample"][0][order], a["x_prompt"][0]])
    o["c_cols"] = np.stack([a["c"][0].reshape(KD, P).T, a["c_ctx"].reshape(KD, P).T], axis=2)
    o["w_ada"] = a["w_ada"]
    o["b_ada_q"] = a["b_ada"].reshape(DEPTH, 3, 4, 512).transpose(0, 2, 1, 3)
    o["norm1_c"] = a["norm1"].reshape(DEPTH, KD, P).transpose(0, 2, 1)
    o["norm2"] = a["norm2"]
    w = a["w_in"]
    at = {"b": 0, "c": 256, "u": 512, "q": 768, "k": 1024}
    tiles = [w[:, :, at[n[0]] + P * int(n[1]):at[n[0]] + P * (int(n[1]) + 1)] for n in PROJ_T]
    wt = np.stack(tiles, 1).reshape(DEPTH, 5, 2, KD, P, P).transpose(0, 1, 4, 2, 3, 5)
    o["w_t"] = wt.reshape(DEPTH, 5, P, 2 * KD * P)
    wn = np.concatenate([w[:, :, 1280:1536], w[:, :, 1792:1952], w[:, :, 1536:1792], w[:, :, 1952:2208]], 2)
    o["w_n"] = wn.reshape(DEPTH, 4, 2, P, 928).transpose(0, 1, 3, 2, 4).reshape(DEPTH, 4, P, 2 * 928)
    o["conv_c"] = a["conv_w"].reshape(DEPTH, 3, 2, P).transpose(0, 3, 2, 1)
    o["rpb_t"] = a["na_rpb"].transpose(0, 1, 3, 2)
    o["gq_c"] = a["mla_gq"].reshape(DEPTH, 2, P).transpose(0, 2, 1)
    for n in ("mla_gkv", "w_fn", "mla_wq_up", "w_out", "w_router", "b_router", "w2"):
        o[n] = a[n]
    o["mla_wkv_up"] = a["mla_wkv_up"].reshape(DEPTH, P, HEADS, 2, HD).transpose(0, 1, 3, 2, 4).reshape(DEPTH, P, 512)
    o["norm_f"] = a["norm_f"].reshape(1, D)
    o["nk_t"] = a["cache_na_k"][0].reshape(DEPTH, 2, 2, P, HD).transpose(0, 2, 4, 1, 3).reshape(DEPTH, P, 2, P)
    o["nv_t"] = a["cache_na_v"][0].transpose(0, 2, 1, 3).reshape(DEPTH, P, 256)
    o["ckv_t"] = a["cache_mla_ckv"][0].transpose(0, 2, 1)
    o["krope_t"] = a["cache_mla_krope"][0].transpose(0, 2, 1)
    w13 = np.concatenate([a["w1"].reshape(DEPTH, NE, KD, P, FF), a["w3"].reshape(DEPTH, NE, KD, P, FF)], 4)
    o["w_13"] = w13.transpose(0, 1, 3, 2, 4).reshape(DEPTH, NE, P, KD * 2 * FF)
    return {k: np.ascontiguousarray(v) for k, v in o.items()}


OUTS = {"y": (N_TOK, D), "nk": (DEPTH, P, 2, P), "nv": (DEPTH, P, 256), "ckv": (DEPTH, P, P), "kr": (DEPTH, P, ROPE)}


def kernel(**inputs):
    import concourse.bacc as bacc
    from concourse.bass_utils import run_bass_kernel_spmd

    nc = bacc.Bacc("TRN2", target_bir_lowering=False, num_devices=1)
    arrays, A, O = {}, {}, {}
    for name, a in {**laid_out(inputs), **shape_constants()}.items():
        arrays[f"in_{name}"] = a
        A[name] = nc.dram_tensor(f"in_{name}", a.shape, mybir.dt.from_np(a.dtype), kind="ExternalInput").ap()
    for name, shape in OUTS.items():
        O[name] = nc.dram_tensor(f"out_{name}", shape, F32, kind="ExternalOutput").ap()
    mixer_kernel(nc, A, O)
    r = run_bass_kernel_spmd(nc, [arrays], core_ids=[0]).results[0]
    y, nk, nv, ckv, kr = (np.asarray(r[f"out_{n}"]) for n in OUTS)
    y_sample = y[0:N_LAT].reshape(GRID_W, GRID_H, D).transpose(1, 0, 2).reshape(1, N_LAT, D)
    new_k = nk.reshape(DEPTH, 2, HD, 2, P).transpose(0, 3, 1, 4, 2).reshape(1, DEPTH, HEADS, P, HD)
    new_v = nv.reshape(DEPTH, P, HEADS, HD).transpose(0, 2, 1, 3).reshape(1, DEPTH, HEADS, P, HD)
    return (y[N_LAT:].reshape(1, N_CTX, D), y_sample, new_k, new_v,
            ckv.reshape(1, DEPTH, P, P), kr.reshape(1, DEPTH, P, ROPE))
```

```python
from contextlib import ExitStack

import numpy as np

import concourse.bass as bass
from concourse import mybir

F32 = mybir.dt.float32
I32 = mybir.dt.int32
ALU = mybir.AluOpType
ACT = mybir.ActivationFunctionType
AX = mybir.AxisListType

P = 128
DEPTH = 2
D = 1024
KD = D // P
N_LAT = 512
N_CTX = 128
N_TOK = N_LAT + N_CTX
GRID_W = 64
GRID_H = N_LAT // GRID_W
TL = N_LAT // P
TT = N_TOK // P
HEADS = 4
HD = 64
NK = 16
N_DC = 31
ROPE = 32
QK = HD + ROPE
NE = 16
FF = 256
EPS = 1e-6
MASKED = -1e30
CREDIT = 2
DVE_CHAIN = 123
BANK = 512
SLOT = 2048
RING = 6

WIN = [0, 64, 192, 256]
BIAS_KIND = [0, 1, 1, 2]
WIN_V = [(0, 1), (6, 7), (7, 8), (2, 3)]
TAB_W = 64
OFF0 = 16


class Signal:

    def __init__(self, sem, per_layer):
        self.sem, self.per_layer = sem, per_layer

    def at(self, layer, n):
        return layer * self.per_layer + n


class PsumPlan:

    def __init__(self):
        self.copies, self.where, self.copied_at, self.cursor, self.count = {}, {}, {}, 0, 0
        self.freed = [0] * 8
        self.last = [None] * 8

    def add(self, key, banks=1, drains=1):
        if banks == 2 and self.cursor % 2:
            self.cursor += 1
        b = self.cursor % 8
        waits = {}
        for c in range(b, b + banks):
            if self.last[c] is not None:
                sem, value = self.last[c]
                waits[sem] = max(waits.get(sem, 0), value)
            else:
                waits[c] = waits.get(c, 0)
                waits[c - c % 2] = waits.get(c - c % 2, 0)
        self.freed[b] += drains
        self.copies[key] = drains
        for c in range(b, b + banks):
            self.last[c] = (b, self.freed[b])
        self.cursor += banks
        self.count += 1
        self.where[key] = (self.count, b, banks, waits)
        self.copied_at[key] = self.freed[b]


def attention_units():
    units = [("na", h, t) for t in range(TL) for h in range(HEADS)]
    units += [("nac", h, TL) for h in range(HEADS)]
    units += [("mlc", h, TL) for h in range(HEADS)]
    units += [("ml", h, t) for h in range(HEADS) for t in range(TL)]
    return units


UNITS = attention_units()
LEAD = 3
WIDTH = {"na": 384, "nac": 128, "mlc": 128, "ml": 640}


def output_after(u):
    kind, h, t = UNITS[u]
    if kind == "ml":
        return ("mlO", h // 2, 0) if h % 2 and t == TL - 1 else None
    return (kind + "O", h // 2, t) if h % 2 else None


def psum_plan():
    plan = PsumPlan()
    plan.add("ada")
    plan.add("modT")
    for k in range(KD):
        plan.add(("h1T", k), 2, 2)
    for m in range(10):
        plan.add(("pT", m), 2)
    for t in range(TT):
        plan.add(("pN", t), 2, 2)
    for cs in range(2):
        plan.add(("fnw", cs))
    for ch in range(2):
        for cs in range(2):
            plan.add(("fnA", ch, cs), 2)
    for kk in range(2):
        plan.add(("cqT", kk), 2)
    plan.add("ckT", 2)
    plan.add("krT", 2, 2)
    for p in range(2):
        plan.add(("kup", p), 2)
    for o in range(2):
        plan.add(("fnY", o), 2)
    for j in range(3):
        plan.add(("vup", j))
    for t in range(TT + 1):
        if t < TT:
            plan.add(("qup", t))
        if t:
            plan.add(("qT", t - 1))
    for step in range(len(UNITS) + LEAD + 1):
        for what, u in steps_at(step):
            kind = UNITS[u][0]
            if what == "S":
                plan.add(("S", u), 2 if kind == "ml" else 1)
            elif what == "T":
                plan.add(("T", u), 2 if kind == "ml" else 1)
            else:
                plan.add(output_after(u))
        if step in MOD_STEPS:
            plan.add(("mod2", MOD_STEPS.index(step)))
    for t in range(TT + 1):
        if t < TT:
            plan.add(("out", t), 2)
        if t:
            plan.add(("h2T", t - 1), 2, 2)
    plan.add("rl", 2)
    plan.add("rT", 2)
    plan.add("rank")
    return plan


def steps_at(step):
    out = []
    if step < len(UNITS):
        out.append(("S", step))
    if 0 <= step - LEAD < len(UNITS):
        out.append(("T", step - LEAD))
    if 0 <= step - LEAD - 1 < len(UNITS) and output_after(step - LEAD - 1):
        out.append(("O", step - LEAD - 1))
    return out


MOD_STEPS = [1, 4, 7, 10, 13, 17, 21, 25]
PROJ_T = ["c0", "u0", "b0", "c1", "u1", "b1", "q0", "q1", "k0", "k1"]
CHUNKS = [("ada", 0, k) for k in range(KD)] + [("wT", m) for m in range(5)] + [("wN", c) for c in range(4)] \
    + [("ada", g, k) for g in (1, 2) for k in range(KD)] + [("wO", c) for c in range(4)]
CHUNK_AT = {c: n for n, c in enumerate(CHUNKS)}
NCH = len(CHUNKS)
SLOT_LOADS = [len(range(s, NCH, RING)) for s in range(RING)]
X13 = [0, 3]
X2 = [2, 5]


def mixer_kernel(nc, A, O):
    plan = psum_plan()
    ctx = ExitStack()
    with ctx:
        top = [0]

        def cut(n):
            top[0] += n
            return top[0] - n

        ARENA = 53060
        arena = ctx.enter_context(nc.sbuf_tensor("arena", [P, ARENA], F32))

        def view(at, *shape, parts=P, p0=0):
            n = int(np.prod(shape))
            v = arena[p0:p0 + parts, at:at + n]
            if len(shape) == 2:
                return v.rearrange("p (a b) -> p a b", a=shape[0])
            if len(shape) == 3:
                return v.rearrange("p (a b c) -> p a b c", a=shape[0], b=shape[1])
            return v

        def ints(name, *shape):
            return ctx.enter_context(nc.sbuf_tensor(name, [P, *shape], I32))

        x = view(cut(TT * D), TT, D)
        at_h = cut(KD * N_TOK)
        hT = view(at_h, KD, N_TOK)
        probsT = view(at_h, 2, 5, N_LAT)
        probsT_s = view(at_h, 4, 3, P)
        h2 = view(at_h, TT, D)
        y_1st = view(at_h, TT, D)
        at_y = cut(KD * N_TOK)
        xn = view(at_y, TT, D)
        yT = view(at_y, KD, N_TOK)
        h2T = view(at_y, KD, N_TOK)
        y_2nd = view(at_y, TT, D)
        at_ring = cut(RING * SLOT)
        slot = [view(at_ring + s * SLOT, SLOT) for s in range(RING)]

        def ring(s, *shape, slots=1):
            return view(at_ring + s * SLOT, *shape)

        ident = view(cut(P), P)
        before = view(cut(P), P)
        ones = view(cut(P), P)
        chan = view(cut(2 * P), 2, P)
        rope = view(cut(2 * TL * 16), 2, TL, 16)
        cond = view(cut(KD * 32), KD, 32)
        w_r = view(cut(KD * 32), KD, 32)
        b_r = view(cut(NE), NE)
        iota16 = view(cut(NE), NE)
        count16 = view(cut(NE), NE)
        count4 = view(cut(4), 4)
        minus_half = view(cut(1), 1)
        limits = view(cut(4), 4)
        n1c = view(cut(KD), KD)
        mod_s = view(cut(2 * KD), 2, KD)
        mod_a = view(cut(2 * KD), 2, KD)
        convw = view(cut(6), 2, 3)
        gq = view(cut(2), 2)
        gkv = view(cut(P), P)
        stat = view(cut(4 * TT), 4, TT)
        rstd = view(cut(4 * TT), 4, TT)
        rowmax = view(cut(4), 4)
        negmax = view(cut(4), 4)
        rowsum = view(cut(4), 4)
        rowinv = view(cut(4), 4)
        gates = view(cut(2 * TT), 2, TT)
        at_a = cut(2 * TL * N_LAT + 2 * P)
        dft = view(at_a, 2, TL, N_LAT)
        dft_c = view(at_a + 2 * TL * N_LAT, 2, P)
        k_m = view(at_a, HEADS, 768)
        cqT = view(at_a + HEADS * 768, 2, N_TOK)
        at_b = cut(4 * N_TOK)
        dftT = view(at_b, 2, 2, N_TOK)
        q_m = view(at_b, HEADS, N_TOK)
        hs = view(at_b, 2, D)
        at_c = cut(2720)
        nat = view(at_c, TT, 512)
        c_sb = view(at_c, N_TOK)
        z_lat = view(at_c + 640, 528)
        z_ctx = view(at_c + 1168, 130)
        cv = view(at_c + 1298, N_TOK)
        masks = view(at_c + 1940, 3, 256)
        probs = view(at_c, 4, 640)
        junk = view(at_c, D)
        hsT_at = at_c
        hid = view(at_c + 2048, 2, FF)
        at_d = cut(HEADS * N_TOK + 2 * 768 + 9 * 256)
        q_n = view(at_d, HEADS, N_TOK)
        k_n = view(at_d + HEADS * N_TOK, 2, 768)
        v_n = view(at_d + HEADS * N_TOK + 2 * 768, 9, 256)
        mods = view(at_d + 2 * D, 512)
        b_ada = view(at_d + 2 * D + 512, 512)
        rows = view(at_d, 3, 2, D)
        at_g = cut(HEADS * 3 * 256)
        bias = view(at_g, HEADS, 3, 256)
        ys = view(at_g, 2, D)
        ff_t = view(at_g + 2 * D, 2, FF)
        at_v = cut(6 * 256)
        w_fn = view(at_v, 2, 256)
        wf = view(at_v + 512, 2, 2, 256)
        v_m = view(at_v, 6, 256)
        ckv_n = view(cut(TT * P), TT, P)
        kr = view(cut(TT * ROPE), TT, ROPE)
        mods2 = view(at_a + HEADS * 768, 2, 512)
        at_up = cut(768)
        ckvT = view(at_up, 768)
        b_ada2 = view(at_up, 2, 512)
        n2q = view(at_up + 1024, 512)
        wq_up = view(cut(768), 2, 384)
        wkv_up = view(cut(512), 512)
        hidT = wq_up[:, 0, 0:256].rearrange("p (a b) -> p a b", a=2)
        hsT = [view(hsT_at, KD, P), view(hsT_at + KD * P, KD, P)]
        q_up = view(at_c, 2, 384)
        tmp4 = view(cut(4 * 64), 4, 64)
        sq_junk = tmp4.rearrange("p a b -> p (a b)")
        c_raw = view(at_g, KD, 2)
        c_exp = view(at_g + 2 * KD, KD, 2)
        zeros = view(at_g + D, D)
        normf_row = view(at_c + D, D)
        r_at = [at_g]

        def rcut(*shape):
            r_at[0] += int(np.prod(shape))
            return view(r_at[0] - int(np.prod(shape)), *shape)

        r_log = rcut(N_TOK)
        r_z = rcut(TT, NE)
        r_s = rcut(TT, NE)
        r_sb = rcut(TT, NE)
        r_pair = rcut(TT * 4, 6)
        r_g = rcut(TT, 4)
        r_gm = rcut(TT)
        r_first = rcut(TT, 4)
        r_m = rcut(TT, NE)
        r_t = rcut(TT, NE)
        r_sel = rcut(2, TT, NE)
        r_mask = rcut(TT, NE)
        r_w = rcut(2, TT)
        r_cum = rcut(TT + 1, NE)
        r_rank = rcut(TT, NE)
        r_pos = rcut(2, TT)
        r_n = rcut(8)
        assert r_at[0] <= at_g + HEADS * 3 * 256, r_at[0] - at_g
        assert top[0] <= ARENA, top[0]
        pos_i = ints("pos_i", 2 * TT)
        rounds_i = ints("rounds_i", 1)
        list_i = ints("list_i", NE, 2)
        idx_i = ints("idx_i", 2)
        out_i = ints("out_i", 2)
        tok_i = ints("tok_i", 2, TT, 2)
        none_i = ints("none_i", 2, 2)

        ps = ctx.enter_context(nc.psum_tensor("ps", [P, 8 * BANK], F32))

        tab = nc.dram_tensor("bias_tab", (HEADS, GRID_H, TAB_W, GRID_H), F32, kind="Internal").ap()
        bias_d = nc.dram_tensor("bias_rows", (P // GRID_H, HEADS, GRID_H, 3, 256), F32, kind="Internal").ap()
        mod_d = nc.dram_tensor("mod_rows", (8, 2, 512), F32, kind="Internal").ap()
        h_d = nc.dram_tensor("expert_in", (N_TOK + 1, D), F32, kind="Internal").ap()
        list_d = nc.dram_tensor("expert_list", (N_TOK * NE, 2), I32, kind="Internal").ap()
        y_d = nc.dram_tensor("expert_out", (2 * N_TOK + 2, D), F32, kind="Internal").ap()
        y_by = y_d[0:2 * N_TOK, :].rearrange("(t p a) d -> t a p d", p=P, a=2)

        def sem(name):
            return ctx.enter_context(nc.semaphore(name))

        def per_layer(name, n):
            return Signal(sem(name), n)

        psum_full = per_layer("psum_full", plan.count)
        psum_copied = [per_layer(f"psum_copied{b}", plan.freed[b]) for b in range(8)]
        chunk_in = [per_layer(f"chunk_in{s}", 16 * SLOT_LOADS[s]) for s in range(RING)]
        chunk_used = per_layer("chunk_used", KD - 1)
        const_in = sem("const_in")
        x_in = sem("x_in")
        passed = sem("passed")
        router_in = sem("router_in")
        dft_in = per_layer("dft_in", 32)
        ada_in = per_layer("ada_in", 16 * 3)
        ada2_in = per_layer("ada2_in", 16 * 2)
        small_in = per_layer("small_in", 16 * 6)
        kv_cache_in = per_layer("kv_cache_in", 16 * 2)
        tab_in = per_layer("tab_in", 16 * GRID_H)
        table_zero = sem("table_zero")
        skewed = per_layer("skewed", 16 * 3)
        bias_in = per_layer("bias_in", 16 * (1 + HEADS))
        krope_in = per_layer("krope_in", 16 * HEADS)
        bias_ready = per_layer("bias_ready", 1)
        cond_exp = sem("cond_exp")
        cond_ready = sem("cond_ready")
        setup_done = sem("setup_done")
        mods_scaled = per_layer("mods_scaled", 1)
        mods_out = per_layer("mods_out", 16)
        gate1_in = per_layer("gate1_in", 16 * 2)
        mod2_in = per_layer("mod2_in", 16 * 4)
        gate2_in = per_layer("gate2_in", 16 * 2)
        squares = per_layer("squares", TT)
        root_x, root_q, root_kv, root_mixed = (per_layer(n, TT) for n in ("root_x", "root_q", "root_kv", "root_mixed"))
        eps_added = sem("eps_added")
        xn_ready = per_layer("xn_ready", TT)
        q_zeroed = per_layer("q_zeroed", 1)
        v_shifted = per_layer("v_shifted", 32)
        kv_squares = per_layer("kv_squares", 2 * TT)
        ckv_raw = per_layer("ckv_raw", TT)
        ckv_ready = per_layer("ckv_ready", TT)
        kr_ready = per_layer("kr_ready", 1)
        caches_out = per_layer("caches_out", 16 * 4)
        q_up_ready = per_layer("q_up_ready", TT)
        NU = len(UNITS)
        max_ready = per_layer("max_ready", NU)
        exp_ready = per_layer("exp_ready", sum(kind == "na" for kind, _, _ in UNITS))
        SMALL = UNITS.index(("ml", 0, 0))
        inv_ready = per_layer("inv_ready", SMALL)
        probs_ready = per_layer("probs_ready", SMALL)
        probs_divided = per_layer("probs_divided", NU - SMALL)
        x_mixed = per_layer("x_mixed", TT)
        squares2 = per_layer("squares2", TT)
        h2_scaled = per_layer("h2_scaled", TT)
        h2_ready = per_layer("h2_ready", TT)
        h2_out = per_layer("h2_out", 16 * TT)
        rexp_ready = per_layer("rexp_ready", 1)
        mask_ready = per_layer("mask_ready", 1)
        routed = per_layer("routed", 1)
        scattered = per_layer("scattered", 16 * 2 * TT)
        list_zeroed = sem("list_zeroed")
        yg_in = [per_layer(f"yg_in{t}", 32) for t in range(TT)]
        y_first = per_layer("y_first", TT)
        x_done = per_layer("x_done", TT)
        cond_step = sem("cond_step")
        y_final = sem("y_final")
        y_out = sem("y_out")
        normf_in = sem("normf_in")
        list_in = sem("list_in")
        list_used = sem("list_used")
        idx_ready = sem("idx_ready")
        place_ready = sem("place_ready")
        hs_in = [sem(f"hs_in{b}") for b in range(2)]
        hsT_full = sem("hsT_full")
        hsT_ready = sem("hsT_ready")
        up_full = sem("up_full")
        e_ready = sem("e_ready")
        hidT_ready = sem("hidT_ready")
        silu_chain = sem("silu_chain")
        hid_ready = sem("hid_ready")
        hidT_full = sem("hidT_full")
        dn_full = sem("dn_full")
        ys_low = sem("ys_low")
        ys_high = sem("ys_high")
        ys_out = [sem(f"ys_out{b}") for b in range(2)]
        x13_in = [sem(f"x13_in{b}") for b in range(2)]
        x2_in = [sem(f"x2_in{b}") for b in range(2)]
        dve_chain = per_layer("dve_chain", DVE_CHAIN)

        block = ctx.enter_context(nc.Block())

        def wait(eng, sem, value):
            eng.wait_ge(sem, value)
            if eng is nc.gpsimd or eng is nc.sync:
                eng.sem_inc(passed, 1)

        def acquire(pe, l, key):
            _, b, banks, waits = plan.where[key]
            for s, value in waits.items():
                pe.wait_ge(psum_copied[s].sem, psum_copied[s].at(l, value))
            return ps[:, b * BANK:(b + banks) * BANK]

        def place(key):
            _, b, banks, _ = plan.where[key]
            return ps[:, b * BANK:(b + banks) * BANK]

        def filled(eng, l, key):
            n, b, banks, _ = plan.where[key]
            wait(eng, psum_full.sem, psum_full.at(l, n))
            return ps[:, b * BANK:(b + banks) * BANK]

        copies = {}

        def bank_of(key):
            copies[key] = copies.get(key, 0) + 1
            return psum_copied[plan.where[key][1]].sem

        def copied(eng, l, *keys):
            need = {}
            for key in keys:
                _, b, _, _ = plan.where[key]
                need[b] = max(need.get(b, 0), plan.copied_at[key])
            for b, value in need.items():
                wait(eng, psum_copied[b].sem, psum_copied[b].at(l, value))
            if eng is nc.tensor:
                eng.sem_inc(passed, 1)

        def used(eng, l, n):
            kind, *i = CHUNKS[n]
            if kind == "ada" and i[0] == 0 and i[1] < KD - 1:
                wait(eng, chunk_used.sem, chunk_used.at(l, i[1] + 1))
            elif kind == "ada":
                filled(eng, l, ("mod2", (i[0] - 1) * 4 + i[1] // 2) if i[0] else "ada")
            else:
                filled(eng, l, {"wT": ("pT", 2 * i[0] + 1), "wN": ("pN", TT - 1),
                                "wO": ("out", TT - 1)}[kind])

        def chunk_wait(pe, l, chunk):
            n = CHUNK_AT[chunk]
            s = n % RING
            pe.wait_ge(chunk_in[s].sem, chunk_in[s].at(l, 16 * (n // RING + 1)))
            return at_ring + s * SLOT

        def by_head(ap, h):
            return ap[:, h * HD:(h + 1) * HD]

        @block.sync
        def _(sp):
            for n, (dst, src) in enumerate([(ident, A["c_ident"]), (before, A["c_before"]), (ones, A["c_ones"]),
                                            (chan, A["c_chan"]), (rope, A["c_rope"]), (b_r, A["b_router"]),
                                            (iota16, A["c_iota"]), (count16, A["c_count"]),
                                            (count4, A["c_count"]), (limits, A["c_limits"])]):
                if n == 5:
                    src = src.rearrange("(a e) -> a e", a=1).broadcast_to((P, NE))
                if n == 8:
                    src = src[:, NE - 4:NE]
                sp.dma_start(dst, src).then_inc(const_in, 16)
            sp.dma_start(tok_i[:, :, :, :], A["c_tok"]).then_inc(const_in, 16)
            for t in range(TT):
                sp.dma_start(x[:, t, :], A["x_all"][t * P:(t + 1) * P, :]).then_inc(x_in, 16)
            sp.dma_start(c_raw, A["c_cols"]).then_inc(x_in, 16)
            done = sp.alloc_register("experts_loaded")
            pair = sp.alloc_register("expert_pair")
            sp.reg_mov(done, 0)
            with sp.Fori(0, DEPTH) as l:
                for n, chunk in enumerate(CHUNKS):
                    s = n % RING
                    if n < RING:
                        if n % 3 != 1:
                            wait(sp, dn_full if n % 3 else up_full,
                                 sp.snap(done, min_val=0, max_val=160) + CREDIT - 1 + n // 3)
                    else:
                        used(sp, l, n - RING)
                    kind, i = chunk[0], chunk[1]
                    dst = slot[s]
                    if kind == "ada":
                        src = A["w_ada"][bass.ds(l, 1), chunk[2] * P:(chunk[2] + 1) * P, i * SLOT:(i + 1) * SLOT]
                        src = src.rearrange("a p n -> (a p) n")
                    elif kind == "wT":
                        src = A["w_t"][bass.ds(l, 1), i].rearrange("a p n -> (a p) n")
                    elif kind == "wN":
                        dst = view(at_ring + s * SLOT, 2 * 928)
                        src = A["w_n"][bass.ds(l, 1), i].rearrange("a p n -> (a p) n")
                    else:
                        dst = ring(s, 2, D)
                        src = A["w_out"][bass.ds(l, 1), i * 2 * P:(i + 1) * 2 * P, :]
                        src = src.rearrange("a (k p) n -> p (a k) n", p=P)
                    sp.dma_start(dst, src).then_inc(chunk_in[s].sem, 16)
                    if chunk == ("ada", 0, KD - 1):
                        sp.dma_start(view(at_a, 2 * TL * N_LAT), A["c_dft"]).then_inc(dft_in.sem, 16)
                        sp.dma_start(view(at_a + 2 * TL * N_LAT, 2 * P), A["c_dft_ctx"]).then_inc(dft_in.sem, 16)
                used(sp, l, NCH - 1)

                def load_expert(e, b):
                    before_it = sp.snap(done, min_val=0, max_val=160) + b
                    wait(sp, up_full, before_it + 1)
                    for half in range(2):
                        sp.dma_start(view(at_ring + (X13[b] + half) * SLOT, SLOT),
                                     A["w_13"][bass.ds(l, 1), bass.ds(e, 1), :, half * SLOT:(half + 1) * SLOT]
                                     .rearrange("a b p n -> (a b p) n")).then_inc(x13_in[b], 16)
                    wait(sp, dn_full, before_it + 1)
                    sp.dma_start(ring(X2[b], 2, D), A["w2"][bass.ds(l, 1), bass.ds(e, 1), :, :]
                                 .rearrange("a b (k p) n -> p (a b k) n", p=P)).then_inc(x2_in[b], 16)

                def expert_rounds():
                    load_expert(0, 0)
                    load_expert(1, 1)
                    wait(sp, routed.sem, routed.at(l, 1))
                    n_rounds = sp.value_load(rounds_i[0:1, 0:1], min_val=1, max_val=5)
                    sp.reg_mov(pair, 0)
                    with sp.Fori(1, n_rounds * (NE // 2)):
                        sp.reg_add(done, done, 2)
                        sp.reg_add(pair, pair, 2)
                        sp.reg_mod(pair, pair, NE)
                        for b in range(2):
                            load_expert(sp.snap(pair, min_val=0, max_val=NE - 2) + b, b)
                    sp.reg_add(done, done, 2)
                expert_rounds()
            wait(sp, x_done.sem, x_done.at(DEPTH, 0))
            sp.dma_start(normf_row, A["norm_f"].broadcast_to((P, D))).then_inc(normf_in, 16)
            wait(sp, y_out, 16 * TT)
            wait(sp, caches_out.sem, caches_out.at(DEPTH, 0))

        @block.gpsimd
        def _(pool):
            pool.memset(w_r, 0.0).then_inc(setup_done, 1)
            pool.memset(none_i[:, :, 0], N_TOK).then_inc(setup_done, 1)
            for b in range(2):
                pool.memset(none_i[:, b, 1:2], 2 * N_TOK + b).then_inc(setup_done, 1)
            pool.memset(minus_half, -0.5)
            pool.memset(zeros, 0.0).then_inc(setup_done, 1)
            pool.wait_ge(setup_done, 5)
            pool.dma_start(w_r[:, :, 0:NE], A["w_router"].rearrange("(k p) e -> p k e", p=P)).then_inc(router_in, 16)
            pool.dma_start(h_d[N_TOK:N_TOK + 1, :], zeros[0:1, :]).then_inc(list_zeroed, 16)

            def empty_lists():
                pool.dma_start(list_d.rearrange("(p n e) a -> p n e a", p=P, e=2),
                               none_i[:, :, :].unsqueeze(1).broadcast_to((P, N_TOK * NE // P // 2, 2, 2)))\
                    .then_inc(list_zeroed, 16)
            empty_lists()
            pool.dma_start(tab.rearrange("h r c k -> (h r) (c k)"), zeros[0:32, 0:TAB_W * GRID_H])\
                .then_inc(table_zero, 16)
            pool.wait_ge(table_zero, 16)
            pool.wait_ge(list_zeroed, 32)
            pool.wait_ge(cond_ready, 1)
            done = pool.alloc_register("experts_done_pool")
            pool.reg_mov(done, 0)

            def inverse_root(n, i, t, root):
                pool.tensor_scalar(stat[:, i, t:t + 1], stat[:, i, t:t + 1], EPS, None, ALU.add).then_inc(eps_added, 1)
                pool.wait_ge(eps_added, n)
                pool.sem_inc(passed, 1)
                pool.tensor_tensor(rstd[:, i, t:t + 1], stat[:, i, t:t + 1], minus_half, ALU.pow).then_inc(root, 1)

            with pool.Fori(0, DEPTH) as l:
                ada_bias = A["b_ada_q"][bass.ds(l, 1)].rearrange("a j (g n) -> (a j) g n", n=512)
                pool.dma_start(b_ada, ada_bias[:, 0, :].unsqueeze(1).broadcast_to((4, 32, 512))).then_inc(ada_in.sem, 16)
                pool.dma_start(n1c, A["norm1_c"][bass.ds(l, 1)].rearrange("a p k -> (a p) k")).then_inc(ada_in.sem, 16)
                pool.dma_start(convw, A["conv_c"][bass.ds(l, 1)].rearrange("a p c w -> (a p) c w")).then_inc(ada_in.sem, 16)
                for t in range(TT):
                    wait(pool, squares.sem, squares.at(l, t + 1))
                    inverse_root(l * 4 * TT + t + 1, 0, t, root_x.sem)
                wait(pool, x_done.sem, x_done.at(l, 0))

                def row(a, lo, n, parts):
                    return a[bass.ds(l, 1), lo:lo + n].broadcast_to((parts, n))

                for r in range(GRID_H):
                    pool.dma_start(tab[:, r, OFF0:OFF0 + N_DC, :],
                                   A["rpb_t"][bass.ds(l, 1), :, :, GRID_H - 1 - r:2 * GRID_H - 1 - r]
                                   .rearrange("a h c k -> (a h) c k")).then_inc(tab_in.sem, 16)
                pool.dma_start(masks, A["c_masks"]).then_inc(bias_in.sem, 16)
                pool.dma_start(gq, A["gq_c"][bass.ds(l, 1)].rearrange("a p k -> (a p) k")).then_inc(small_in.sem, 16)
                pool.dma_start(gkv, row(A["mla_gkv"], 0, P, P)).then_inc(small_in.sem, 16)
                pool.dma_start(w_fn, A["w_fn"][bass.ds(l, 1)].rearrange("a (k p) n -> p (a k) n", p=P)).then_inc(small_in.sem, 16)
                pool.dma_start(wq_up, A["mla_wq_up"][bass.ds(l, 1)].rearrange("a (k p) n -> p (a k) n", p=P)).then_inc(small_in.sem, 16)
                pool.dma_start(wkv_up, A["mla_wkv_up"][bass.ds(l, 1)].rearrange("a p n -> (a p) n")).then_inc(small_in.sem, 16)
                pool.dma_start(ckvT[:, 512:640], A["ckv_t"][bass.ds(l, 1)].rearrange("a p n -> (a p) n")).then_inc(small_in.sem, 16)
                wait(pool, tab_in.sem, tab_in.at(l, 16 * GRID_H))
                for kind in range(3):
                    first = OFF0 + 15 - 8 * kind
                    src = bass.AP(tensor=tab.tensor, offset=first * GRID_H,
                                  ap=[[GRID_H * TAB_W * GRID_H, HEADS], [TAB_W * GRID_H, GRID_H], [-GRID_H, 16], [1, 256]])
                    pool.dma_start(bias_d[:, :, :, kind, :].rearrange("c h r n -> h r c n"), src)\
                        .then_inc(skewed.sem, 16)
                wait(pool, skewed.sem, skewed.at(l, 16 * 3))
                for h in range(HEADS):
                    pool.dma_start(bias[:, h, :, :], bias_d[:, h].rearrange("c r k n -> c r (k n)")).then_inc(bias_in.sem, 16)
                wait(pool, bias_in.sem, bias_in.at(l, bias_in.per_layer))
                for h in range(HEADS):
                    ins = pool.tensor_tensor(bias[:, h, :, :], bias[:, h, :, :], masks, ALU.add)
                ins.then_inc(bias_ready.sem, 1)
                copied(pool, l, "modT")
                pool.memset(q_n, 0.0).then_inc(q_zeroed.sem, 1)
                wait(pool, q_zeroed.sem, q_zeroed.at(l, 1))
                pool.dma_start(k_n[:, :, 512:640], A["nk_t"][bass.ds(l, 1)].rearrange("a p k n -> (a p) k n")).then_inc(kv_cache_in.sem, 16)
                pool.dma_start(v_n[:, 5, :], A["nv_t"][bass.ds(l, 1)].rearrange("a p n -> (a p) n")).then_inc(kv_cache_in.sem, 16)
                for t in range(TT):
                    wait(pool, kv_squares.sem, kv_squares.at(l, 2 * t + 2))
                    inverse_root(l * 4 * TT + TT + 2 * t + 1, 1, t, root_q.sem)
                    inverse_root(l * 4 * TT + TT + 2 * t + 2, 2, t, root_kv.sem)
                copied(pool, l, *[("pN", t) for t in range(TT)])
                pool.dma_start(v_n[0:64, 6:9, :], v_n[64:128, 0:3, :]).then_inc(v_shifted.sem, 16)
                pool.dma_start(v_n[64:128, 6:9, :], v_n[0:64, 1:4, :]).then_inc(v_shifted.sem, 16)
                copied(pool, l, ("pT", 8), ("pT", 9))
                wait(pool, ckv_ready.sem, ckv_ready.at(l, TT))
                wait(pool, kr_ready.sem, kr_ready.at(l, 1))
                for n, (dst, src) in enumerate([(O["nk"], k_n[:, :, 640:768]), (O["nv"], v_n[:, 4, :]),
                                                (O["ckv"], ckv_n[:, TL, :]), (O["kr"], kr[:, TL, :])]):
                    dst = dst[bass.ds(l, 1)]
                    dst = dst.rearrange("a p k n -> (a p) k n") if n == 0 else dst.rearrange("a p n -> (a p) n")
                    pool.dma_start(dst, src).then_inc(caches_out.sem, 16)
                filled(pool, l, ("fnA", 1, 1))
                for h in range(HEADS):
                    pool.dma_start(k_m[64:96, h, 512:640], A["krope_t"][bass.ds(l, 1)].rearrange("a p n -> (a p) n")).then_inc(krope_in.sem, 16)
                filled(pool, l, ("qT", TT - 1))
                pool.dma_start(b_ada2, ada_bias[:, 1:3, :].rearrange("j g n -> j (g n)").unsqueeze(1)
                               .broadcast_to((4, 32, 1024))).then_inc(ada2_in.sem, 16)
                pool.dma_start(n2q[0:64, :], A["norm2"][bass.ds(l, 1)].rearrange("a (j n) -> (a j) n", j=2)
                               .unsqueeze(1).broadcast_to((2, 32, 512))).then_inc(ada2_in.sem, 16)

                def mod_row(g, half, c):
                    return mod_d.rearrange("(j c) g n -> c g j n", c=2)[c, g, 2 * half:2 * half + 2, :]\
                        .unsqueeze(0).broadcast_to((P, 2, 512))

                for u, (kind, h, t) in enumerate(UNITS[:SMALL]):
                    wait(pool, inv_ready.sem, inv_ready.at(l, u + 1))
                    pr = probs[:, u % 4, 0:WIDTH[kind]]
                    pool.tensor_scalar(pr, pr, rowinv[:, u % 4:u % 4 + 1], None, ALU.mult).then_inc(probs_ready.sem, 1)
                wait(pool, mods_scaled.sem, mods_scaled.at(l, 1))
                pool.dma_start(mod_d, mods2[0:P:16, :, :]).then_inc(mods_out.sem, 16)
                wait(pool, mods_out.sem, mods_out.at(l, 16))
                wait(pool, caches_out.sem, caches_out.at(l, 64))
                filled(pool, l, ("nacO", 1, TL))
                for n, (g, half) in enumerate([(0, 0), (1, 0), (0, 1)]):
                    for c in range(2):
                        pool.dma_start(rows[:, n, c, :].rearrange("p (j n) -> p j n", j=2), mod_row(g, half, c))\
                            .then_inc((gate1_in if n == 0 else mod2_in).sem, 16)
                for t in range(TT):
                    wait(pool, squares2.sem, squares2.at(l, t + 1))
                    inverse_root(l * 4 * TT + 3 * TT + t + 1, 3, t, root_mixed.sem)
                    wait(pool, h2_scaled.sem, h2_scaled.at(l, t + 1))
                    if t == 0:
                        wait(pool, mod2_in.sem, mod2_in.at(l, 64))
                    pool.tensor_tensor(h2[:, t, :], h2[:, t, :], rows[:, 2, t // TL, :], ALU.add).then_inc(h2_ready.sem, 1)
                    wait(pool, h2_ready.sem, h2_ready.at(l, t + 1))
                    pool.dma_start(h_d[t * P:(t + 1) * P, :], h2[:, t, :]).then_inc(h2_out.sem, 16)
                wait(pool, x_mixed.sem, x_mixed.at(l, TT))
                for c in range(2):
                    pool.dma_start(rows[:, 0, c, :].rearrange("p (j n) -> p j n", j=2), mod_row(1, 1, c))\
                        .then_inc(gate2_in.sem, 16)
                wait(pool, routed.sem, routed.at(l, 1))
                wait(pool, list_zeroed, l * 16 + 32)
                for a in range(2):
                    for t in range(TT):
                        pool.indirect_dma_start(
                            out=list_d, out_offset=bass.IndirectOffsetOnAxis(ap=pos_i[:, a * TT + t:a * TT + t + 1], axis=0),
                            in_=tok_i[:, a, t, :], in_offset=None).then_inc(scattered.sem, 16)
                wait(pool, scattered.sem, scattered.at(l, 16 * 2 * TT))
                wait(pool, h2_out.sem, h2_out.at(l, 16 * TT))

                def rounds():
                    n_rounds = pool.value_load(rounds_i[0:1, 0:1], min_val=1, max_val=5)
                    with pool.Fori(0, n_rounds) as r:
                        base = pool.snap(done, min_val=0, max_val=160)
                        wait(pool, hs_in[1], base * 8)
                        wait(pool, place_ready, base)
                        pool.dma_start(list_i[:, :, :].rearrange("p e a -> p (e a)"),
                                       list_d.rearrange("(k e) a -> k (e a)", e=NE)[bass.ds(r * P, P), :])\
                            .then_inc(list_in, 16)
                        wait(pool, list_in, base + 16)

                        def gather(e, b):
                            wait(pool, hs_in[b], base * 8 + (e - b) * 8)
                            pool.tensor_copy(idx_i[:, b:b + 1], list_i[:, bass.ds(e, 1), 0]).then_inc(idx_ready, 1)
                            wait(pool, idx_ready, base + e + 1)
                            wait(pool, hsT_full, base + e + 1)
                            pool.indirect_dma_start(
                                out=hs[:, b, :], out_offset=None, in_=h_d,
                                in_offset=bass.IndirectOffsetOnAxis(ap=idx_i[:, b:b + 1], axis=0)).then_inc(hs_in[b], 16)

                        def scatter(e, b):
                            wait(pool, ys_out[b], base * 8 + (e - b) * 8)
                            pool.tensor_copy(out_i[:, b:b + 1], list_i[:, bass.ds(e, 1), 1]).then_inc(place_ready, 1)
                            wait(pool, place_ready, base + e + 1)
                            wait(pool, ys_low, base + e + 1 + CREDIT)
                            wait(pool, ys_high, base + e + 1 + CREDIT)
                            pool.indirect_dma_start(
                                out=y_d, out_offset=bass.IndirectOffsetOnAxis(ap=out_i[:, b:b + 1], axis=0),
                                in_=ys[:, b, :], in_offset=None).then_inc(ys_out[b], 16)

                        for e in range(3):
                            gather(e, e % 2)
                        with pool.Fori(0, NE // 2 - 2) as i:
                            gather(2 * i + 3, 1)
                            scatter(2 * i, 0)
                            gather(2 * i + 4, 0)
                            scatter(2 * i + 1, 1)
                        gather(NE - 1, 1)
                        for e in range(NE - 4, NE):
                            scatter(e, e % 2)
                        pool.reg_add(done, done, NE)
                rounds()
                empty_lists()
            for t in range(TT):
                pool.wait_ge(squares.sem, squares.at(DEPTH, t + 1))
                inverse_root(DEPTH * 4 * TT + t + 1, 0, t, root_x.sem)
            pool.wait_ge(list_zeroed, 32 + 16 * DEPTH)

        @block.tensor
        def _(pe):
            mm, tr = pe.matmul, pe.transpose
            for s in (hsT_full, up_full, dn_full):
                pe.sem_inc(s, CREDIT)
            pe.sem_inc(ys_low, CREDIT)
            pe.sem_inc(ys_high, CREDIT)
            pe.wait_ge(const_in, 16 * 11)
            pe.wait_ge(router_in, 16)
            pe.wait_ge(cond_ready, 1)
            done = pe.alloc_register("experts_done_pe")
            pe.reg_mov(done, 0)

            def both(out, lhsT, rhs_of, k, n):
                mm(out[:, 0:N_LAT], lhsT, rhs_of[:, 0:N_LAT], start=(k == 0), stop=(k == n - 1))
                return mm(out[:, N_LAT:N_TOK], lhsT, rhs_of[:, N_LAT:N_TOK], start=(k == 0), stop=(k == n - 1))

            with pe.Fori(0, DEPTH) as l:
                def modulation(out, g, ks):
                    for k in ks:
                        w = view(chunk_wait(pe, l, ("ada", g, k)), 4, 512)
                        for j in range(4):
                            ins = mm(out[32 * j:32 * j + 32, 0:512], cond[:, k, :], w[:, j, :],
                                     start=(k == ks[0]), stop=(k == ks[-1]), skip_group_check=True)
                        if k != ks[-1] and g == 0:
                            ins.then_inc(chunk_used.sem, 1)
                    ins.then_inc(psum_full.sem, 1)

                modulation(acquire(pe, l, "ada"), 0, range(KD))
                copied(pe, l, "ada")
                out = acquire(pe, l, "modT")
                for i in range(4):
                    ins = tr(out[:, i * P:(i + 1) * P], mods[:, i * P:(i + 1) * P], ident)
                ins.then_inc(psum_full.sem, 1)
                for k in range(KD):
                    out = acquire(pe, l, ("h1T", k))
                    for t in range(TT):
                        pe.wait_ge(xn_ready.sem, xn_ready.at(l, t + 1)) if k == 0 else None
                        ins = tr(out[:, t * P:(t + 1) * P], xn[:, t, k * P:(k + 1) * P], ident)
                    ins.then_inc(psum_full.sem, 1)
                copied(pe, l, *[("h1T", k) for k in range(KD)])
                for m in range(10):
                    w = view(chunk_wait(pe, l, ("wT", m // 2)), 2, KD, P)
                    out = acquire(pe, l, ("pT", m))
                    for k in range(KD):
                        ins = both(out, w[:, m % 2, k, :], hT[:, k, :], k, KD)
                    ins.then_inc(psum_full.sem, 1)
                w = [view(chunk_wait(pe, l, ("wN", c)), 2, 928) for c in range(4)]
                for t in range(TT):
                    out = acquire(pe, l, ("pN", t))
                    for k in range(KD):
                        hk = hT[:, k, t * P:(t + 1) * P]
                        mm(out[:, 0:416], hk, w[k // 2][:, k % 2, 0:416], start=(k == 0), stop=(k == KD - 1))
                        ins = mm(out[:, 512:1024], hk, w[k // 2][:, k % 2, 416:928], start=(k == 0), stop=(k == KD - 1))
                    ins.then_inc(psum_full.sem, 1)
                pe.wait_ge(small_in.sem, small_in.at(l, small_in.per_layer))
                for cs in range(2):
                    out = acquire(pe, l, ("fnw", cs))
                    for kk in range(2):
                        ins = mm(out[:, kk * 256:(kk + 1) * 256], chan[:, cs, :], w_fn[:, kk, :],
                                 start=True, stop=True, skip_group_check=True)
                    ins.then_inc(psum_full.sem, 1)
                pe.wait_ge(dft_in.sem, dft_in.at(l, 32))
                copied(pe, l, *[("pN", t) for t in range(TT)])
                for ch in range(2):
                    for cs in range(2):
                        out = acquire(pe, l, ("fnA", ch, cs))
                        lo = 256 + ch * P
                        for t in range(TL):
                            mm(out[:, 0:N_LAT], nat[:, t, lo:lo + P], dft[:, cs, t, :], start=(t == 0), stop=(t == TL - 1))
                        mm(out[:, N_LAT:N_TOK], nat[:, TL, lo:lo + P], dft_c[:, cs, :], start=True, stop=True)\
                            .then_inc(psum_full.sem, 1)
                for kk in range(2):
                    out = acquire(pe, l, ("cqT", kk))
                    for t in range(TT):
                        ins = tr(out[:, t * P:(t + 1) * P], nat[:, t, kk * P:(kk + 1) * P], ident)
                    ins.then_inc(psum_full.sem, 1)
                out = acquire(pe, l, "ckT")
                pe.wait_ge(ckv_ready.sem, ckv_ready.at(l, TT))
                for t in range(TT):
                    ins = tr(out[:, t * P:(t + 1) * P], ckv_n[:, t, :], ident)
                ins.then_inc(psum_full.sem, 1)
                out = acquire(pe, l, "krT")
                pe.wait_ge(kr_ready.sem, kr_ready.at(l, 1))
                for t in range(TT):
                    ins = tr(out[0:ROPE, t * P:(t + 1) * P], kr[:, t, :], ident)
                ins.then_inc(psum_full.sem, 1)
                copied(pe, l, "ckT", ("fnw", 0), ("fnw", 1), *[("fnA", ch, cs) for ch in range(2) for cs in range(2)])
                for p in range(2):
                    out = acquire(pe, l, ("kup", p))
                    w = wkv_up[:, p * P:(p + 1) * P]
                    mm(out[:, 0:512], w, ckvT[:, 0:512], start=True, stop=True)
                    mm(out[:, 512:768], w, ckvT[:, 512:768], start=True, stop=True).then_inc(psum_full.sem, 1)
                for o in range(2):
                    out = acquire(pe, l, ("fnY", o))
                    for n in range(4):
                        ins = both(out, wf[:, n // 2, n % 2, o * P:(o + 1) * P], dftT[:, n // 2, n % 2, :], n, 4)
                    ins.then_inc(psum_full.sem, 1)
                for j in range(3):
                    out = acquire(pe, l, ("vup", j))
                    for n in range(2):
                        c = 2 * j + n
                        ins = mm(out[:, n * 256:(n + 1) * 256], ckvT[:, c * P:(c + 1) * P], wkv_up[:, 256:512],
                                 start=True, stop=True, skip_group_check=True)
                    ins.then_inc(psum_full.sem, 1)
                copied(pe, l, ("cqT", 0), ("cqT", 1))
                for t in range(TT + 1):
                    if t < TT:
                        out = acquire(pe, l, ("qup", t))
                        for kk in range(2):
                            ins = mm(out[:, 0:384], cqT[:, kk, t * P:(t + 1) * P], wq_up[:, kk, :],
                                     start=(kk == 0), stop=(kk == 1))
                        ins.then_inc(psum_full.sem, 1)
                    if t:
                        out = acquire(pe, l, ("qT", t - 1))
                        pe.wait_ge(q_up_ready.sem, q_up_ready.at(l, t))
                        for h in range(HEADS):
                            ins = tr(out[0:QK, h * P:(h + 1) * P], q_up[:, (t - 1) % 2, h * QK:(h + 1) * QK], ident)
                        ins.then_inc(psum_full.sem, 1)
                pe.wait_ge(kv_cache_in.sem, kv_cache_in.at(l, 32))
                pe.wait_ge(v_shifted.sem, v_shifted.at(l, 32))
                pe.wait_ge(krope_in.sem, krope_in.at(l, 16 * HEADS))
                copied(pe, l, *[("pT", m) for m in range(6, 10)], "krT", *[("kup", p) for p in range(2)],
                       *[("qT", t) for t in range(TT)], *[("vup", j) for j in range(3)])
                for step in range(len(UNITS) + LEAD + 1):
                    for what, u in steps_at(step):
                        kind, h, t = UNITS[u]
                        p = h // 2
                        cols = slice(t * P, (t + 1) * P)
                        if what == "S":
                            out = acquire(pe, l, ("S", u))
                            if kind == "na":
                                mm(out[:, 0:256], q_n[:, h, cols], k_n[:, p, WIN[t]:WIN[t] + 256], start=True, stop=True,
                                   skip_group_check=True)
                                ins = mm(out[:, 256:384], q_n[:, h, cols], k_n[:, p, 512:640], start=True, stop=True,
                                         skip_group_check=True)
                            elif kind == "nac":
                                ins = mm(out[:, 0:P], q_n[:, h, cols], k_n[:, p, 640:768], start=True, stop=True)
                            elif kind == "mlc":
                                ins = mm(out[:, 0:P], q_m[0:QK, h, cols], k_m[0:QK, h, 640:768], start=True, stop=True)
                            else:
                                mm(out[:, 0:512], q_m[0:QK, h, cols], k_m[0:QK, h, 0:512], start=True, stop=True)
                                ins = mm(out[:, 512:640], q_m[0:QK, h, cols], k_m[0:QK, h, 512:640], start=True, stop=True)
                            ins.then_inc(psum_full.sem, 1)
                        elif what == "T":
                            out = acquire(pe, l, ("T", u))
                            if u < SMALL:
                                pe.wait_ge(probs_ready.sem, probs_ready.at(l, u + 1))
                            else:
                                pe.wait_ge(probs_divided.sem, probs_divided.at(l, u + 1 - SMALL))
                            for c in range(WIDTH[kind] // P):
                                ins = tr(out[:, c * P:(c + 1) * P], probs[:, u % 4, c * P:(c + 1) * P], ident)
                            ins.then_inc(psum_full.sem, 1)
                        else:
                            key = output_after(u)
                            copied(pe, l, ("T", u - 1), ("T", u))
                            out = acquire(pe, l, key)
                            if kind == "ml":
                                steps = [(probsT[:, hh % 2, c, :], v_m[:, c, :], c) for c in range(5) for hh in (h - 1, h)]
                                n, width = 5, N_LAT
                            elif kind == "na":
                                vs = (*WIN_V[t], 5)
                                steps = [(probsT_s[:, (u - 1 + i) % 4, c, :], v_n[:, vs[c], :], c) for c in range(3) for i in range(2)]
                                n, width = 3, P
                            else:
                                v = v_n[:, 4, :] if kind == "nac" else v_m[:, 5, :]
                                steps = [(probsT_s[:, (u - 1 + i) % 4, 0, :], v, 0) for i in range(2)]
                                n, width = 1, P
                            for i, (pt, v, c) in enumerate(steps):
                                hh = 2 * p + i % 2
                                lo = 64 * (i % 2)
                                ins = mm(out[lo:lo + 64, 0:width], by_head(v, hh), pt, start=(c == 0), stop=(c == n - 1),
                                         skip_group_check=True)
                            ins.then_inc(psum_full.sem, 1)
                    if step in MOD_STEPS:
                        i = MOD_STEPS.index(step)
                        modulation(acquire(pe, l, ("mod2", i)), 1 + i // 4, range(2 * (i % 4), 2 * (i % 4) + 2))
                copied(pe, l, ("pT", 2), ("pT", 5), ("fnY", 0), ("fnY", 1),
                       *[output_after(u) for u in range(len(UNITS)) if output_after(u)])
                w = [view(chunk_wait(pe, l, ("wO", c)), 2, D) for c in range(4)]
                def experts_input(t):
                    out = acquire(pe, l, ("h2T", t))
                    pe.wait_ge(h2_ready.sem, h2_ready.at(l, t + 1))
                    for k in range(KD):
                        ins = tr(out[:, k * P:(k + 1) * P], h2[:, t, k * P:(k + 1) * P], ident)
                    ins.then_inc(psum_full.sem, 1)

                for t in range(TT):
                    out = acquire(pe, l, ("out", t))
                    for k in range(KD):
                        for n in range(2):
                            ins = mm(out[:, n * 512:(n + 1) * 512], yT[:, k, t * P:(t + 1) * P],
                                     w[k // 2][:, k % 2, n * 512:(n + 1) * 512], start=(k == 0), stop=(k == KD - 1))
                    ins.then_inc(psum_full.sem, 1)
                    if t:
                        experts_input(t - 1)
                copied(pe, l, *[("h2T", t) for t in range(TL)])
                router_out = acquire(pe, l, "rl")
                for k in range(KD):
                    j = k % 4
                    mm(router_out[32 * j:32 * j + 32, 0:N_LAT], w_r[:, k, :], h2T[:, k, 0:N_LAT], start=(k < 4), stop=(k >= 4),
                       skip_group_check=True)
                experts_input(TL)
                copied(pe, l, ("h2T", TL))
                out = router_out
                for k in range(KD):
                    j = k % 4
                    ins = mm(out[32 * j:32 * j + 32, N_LAT:N_TOK], w_r[:, k, :], h2T[:, k, N_LAT:N_TOK], start=(k < 4), stop=(k >= 4),
                             skip_group_check=True)
                ins.then_inc(psum_full.sem, 1)
                copied(pe, l, "rl")
                out = acquire(pe, l, "rT")
                for t in range(TT):
                    ins = tr(out[:, t * P:(t + 1) * P], r_log[:, t * P:(t + 1) * P], ident)
                ins.then_inc(psum_full.sem, 1)
                out = acquire(pe, l, "rank")
                pe.wait_ge(mask_ready.sem, mask_ready.at(l, 1))
                m80 = r_mask.rearrange("p a b -> p (a b)")
                mm(out[:, 0:80], before, m80, start=True, stop=True, skip_group_check=True)
                mm(out[:, 128:208], ones, m80, start=True, stop=True, skip_group_check=True).then_inc(psum_full.sem, 1)
                for b in range(8):
                    pe.wait_ge(psum_copied[b].sem, psum_copied[b].at(l, plan.freed[b]))

                def tokens(base, e, b):
                    pe.wait_ge(hs_in[b], base * 8 + (e - b) * 8 + 16)
                    pe.wait_ge(hsT_ready, base * 2 + e * 2)
                    for k in range(KD):
                        ins = tr(ps[:, k * P:(k + 1) * P], hs[:, b, k * P:(k + 1) * P], ident)
                    ins.then_inc(hsT_full, 1)

                def up(base, e, b):
                    pe.wait_ge(x13_in[b], base * 16 + (e - b) * 16 + 32)
                    pe.wait_ge(hsT_ready, base * 2 + e * 2 + 2)
                    w = view(at_ring + X13[b] * SLOT, KD, 2 * FF)
                    out = ps[:, (2 + b) * BANK:(3 + b) * BANK]
                    for k in range(KD):
                        ins = mm(out, hsT[b][:, k, :], w[:, k, :], start=(k == 0), stop=(k == KD - 1))
                    ins.then_inc(up_full, 1)

                def hidden(base, e, b):
                    pe.wait_ge(hid_ready, base + e + 1)
                    for f in range(2):
                        ins = tr(ps[:, (2 + b) * BANK + f * P:(2 + b) * BANK + (f + 1) * P], hid[:, b, f * P:(f + 1) * P], ident)
                    ins.then_inc(hidT_full, 1)

                def down(base, e, b):
                    pe.wait_ge(x2_in[b], base * 8 + (e - b) * 8 + 16)
                    pe.wait_ge(hidT_ready, base + e + 1)
                    pe.wait_ge(ys_low, base + e + 1)
                    pe.wait_ge(ys_high, base + e + 1)
                    w = ring(X2[b], 2, D)
                    out = ps[:, (4 + 2 * b) * BANK:(6 + 2 * b) * BANK]
                    for n in range(2):
                        for f in range(2):
                            ins = mm(out[:, n * 512:(n + 1) * 512], hidT[:, f, :], w[:, f, n * 512:(n + 1) * 512],
                                     start=(f == 0), stop=(f == 1))
                    ins.then_inc(dn_full, 1)

                def rounds():
                    pe.wait_ge(routed.sem, routed.at(l, 1))
                    pe.sem_inc(passed, 1)
                    n_rounds = pe.value_load(rounds_i[0:1, 0:1], min_val=1, max_val=5)
                    with pe.Fori(0, n_rounds):
                        base = pe.snap(done, min_val=0, max_val=160)
                        for e in range(2):
                            tokens(base, e, e)
                            up(base, e, e)
                        with pe.Fori(0, NE // 2 - 1) as i:
                            for b in range(2):
                                hidden(base, 2 * i + b, b)
                                tokens(base, 2 * i + 2 + b, b)
                                down(base, 2 * i + b, b)
                                up(base, 2 * i + 2 + b, b)
                        for b in range(2):
                            hidden(base, NE - 2 + b, b)
                            down(base, NE - 2 + b, b)
                        pe.reg_add(done, done, NE)
                rounds()

        @block.scalar
        def _(act):
            act.wait_ge(x_in, 16 * (TT + 1))
            act.activation(c_exp, c_raw, ACT.Exp, scale=-1.0).then_inc(cond_exp, 1)
            done = act.alloc_register("experts_done_act")
            act.reg_mov(done, 0)

            def mean_square(n, t):
                if n is not None:
                    act.wait_ge(squares.sem, n)
                act.activation(junk, x[:, t, :], ACT.Square, scale=D ** -0.5,
                               accum_out=stat[:, 0, t:t + 1]).then_inc(squares.sem, 1)

            for t in range(TT):
                mean_square(t or None, t)
            with act.Fori(0, DEPTH) as l:
                copied(act, l, "modT")
                for k in range(KD):
                    out = filled(act, l, ("h1T", k))
                    act.activation(hT[:, k, N_LAT:N_TOK], out[:, N_LAT:N_TOK], ACT.Identity,
                                   scale=mod_a[:, 1, k:k + 1], bias=mod_s[:, 1, k:k + 1]).then_inc(bank_of(("h1T", k)), 1)
                act.wait_ge(bias_ready.sem, bias_ready.at(l, 1))
                for c in range(2):
                    out = filled(act, l, ("pT", 3 * c))
                    if c == 1:
                        copied(act, l, ("pT", 1))
                    act.activation(c_sb, out[:, 0:N_TOK], ACT.Copy).then_inc(bank_of(("pT", 3 * c)), 1)
                act.wait_ge(q_zeroed.sem, q_zeroed.at(l, 1))
                for p in range(2):
                    out = filled(act, l, ("pT", 6 + p))
                    act.activation(q_n[0:64, 2 * p, :], out[0:64, 0:N_TOK], ACT.Copy)
                    act.activation(q_n[64:128, 2 * p + 1, :], out[64:128, 0:N_TOK], ACT.Copy).then_inc(bank_of(("pT", 6 + p)), 1)
                copied(act, l, ("pT", 2), ("pT", 5))
                for t in range(TT):
                    out = filled(act, l, ("pN", t))
                    act.wait_ge(kv_squares.sem, kv_squares.at(l, 2 * t))
                    act.activation(sq_junk, out[:, 512:768], ACT.Square, scale=256 ** -0.5,
                                   accum_out=stat[:, 1, t:t + 1]).then_inc(kv_squares.sem, 1)
                    act.activation(nat[:, t, :], out[:, 512:1024], ACT.Copy).then_inc(bank_of(("pN", t)), 1)
                    act.wait_ge(ckv_raw.sem, ckv_raw.at(l, t + 1))
                    act.wait_ge(kv_squares.sem, kv_squares.at(l, 2 * t + 1))
                    act.activation(sq_junk[:, 0:P], ckv_n[:, t, :], ACT.Square, scale=P ** -0.5,
                                   accum_out=stat[:, 2, t:t + 1]).then_inc(kv_squares.sem, 1)
                act.wait_ge(small_in.sem, small_in.at(l, small_in.per_layer))
                for cs in range(2):
                    out = filled(act, l, ("fnw", cs))
                    act.activation(wf[:, cs, :, :], out[:, 0:512].rearrange("p (a b) -> p a b", a=2), ACT.Copy)\
                        .then_inc(bank_of(("fnw", cs)), 1)
                for ch in range(2):
                    out = filled(act, l, ("fnA", ch, 1))
                    act.activation(dftT[:, 1, ch, :], out[:, 0:N_TOK], ACT.Copy).then_inc(bank_of(("fnA", ch, 1)), 1)
                for kk in range(2):
                    out = filled(act, l, ("cqT", kk))
                    act.activation(cqT[:, kk, :], out[:, 0:N_TOK], ACT.Copy, scale=gq[:, kk:kk + 1])\
                        .then_inc(bank_of(("cqT", kk)), 1)
                out = filled(act, l, "krT")
                for h in range(HEADS):
                    ins = act.activation(k_m[64:96, h, 0:N_LAT], out[0:ROPE, 0:N_LAT], ACT.Copy)
                ins.then_inc(bank_of("krT"), 1)
                for p in range(2):
                    out = filled(act, l, ("kup", p))
                    act.activation(k_m[0:64, 2 * p, :], out[0:64, 0:768], ACT.Copy)
                    act.activation(k_m[0:64, 2 * p + 1, :], out[64:128, 0:768], ACT.Copy).then_inc(bank_of(("kup", p)), 1)
                for j in range(3):
                    out = filled(act, l, ("vup", j))
                    act.activation(v_m[:, 2 * j:2 * j + 2, :], out[:, 0:512].rearrange("p (a b) -> p a b", a=2), ACT.Copy)\
                        .then_inc(bank_of(("vup", j)), 1)
                for t in range(TT):
                    out = filled(act, l, ("qup", t))
                    act.wait_ge(root_q.sem, root_q.at(l, t + 1))
                    act.activation(q_up[:, t % 2, :], out[:, 0:384], ACT.Copy, scale=rstd[:, 1, t:t + 1])\
                        .then_inc(bank_of(("qup", t)), 1)
                for step in range(len(UNITS) + LEAD):
                    if step < len(UNITS):
                        u = step
                        kind, h, t = UNITS[u]
                        out = filled(act, l, ("S", u))
                        pr = probs[:, u % 4, 0:WIDTH[kind]]
                        if kind == "na":
                            act.wait_ge(max_ready.sem, max_ready.at(l, u + 1))
                            act.activation(pr, pr, ACT.Exp, bias=negmax[:, u % 4:u % 4 + 1],
                                           accum_out=rowsum[:, u % 4:u % 4 + 1]).then_inc(exp_ready.sem, 1)
                        else:
                            act.wait_ge(max_ready.sem, max_ready.at(l, u + 1))
                            act.activation(pr, out[:, 0:WIDTH[kind]], ACT.Exp, bias=negmax[:, u % 4:u % 4 + 1],
                                           scale=(HD if kind == "nac" else QK) ** -0.5,
                                           accum_out=rowsum[:, u % 4:u % 4 + 1]).then_inc(bank_of(("S", u)), 1)
                    if step >= LEAD:
                        u = step - LEAD
                        kind, h, t = UNITS[u]
                        last = {24: ("mlcO", 1, TL), 32: ("mlO", 0, 0)}.get(u, ("T", u))
                        filled(act, l, last)
                        out = place(("T", u))
                        wd = WIDTH[kind]
                        src = out[:, 0:wd].rearrange("p (a b) -> p a b", a=wd // P)
                        if kind == "ml":
                            dst = probsT[:, h % 2, :, t * P:(t + 1) * P]
                        else:
                            dst = probsT_s[:, u % 4, 0:wd // P, :]
                        act.activation(dst, src, ACT.Copy).then_inc(bank_of(("T", u)), 1)
                for t in range(TT):
                    act.wait_ge(x_mixed.sem, x_mixed.at(l, t + 1))
                    act.wait_ge(squares2.sem, squares2.at(l, t))
                    act.activation(junk, x[:, t, :], ACT.Square, scale=D ** -0.5,
                                   accum_out=stat[:, 3, t:t + 1]).then_inc(squares2.sem, 1)
                    for t2 in {0: (), TL: (TL - 1, TL)}.get(t, (t - 1,)):
                        out = filled(act, l, ("h2T", t2))
                        act.activation(h2T[:, 4:8, t2 * P:(t2 + 1) * P], out[:, 512:1024].rearrange("p (k n) -> p k n", k=4),
                                       ACT.Copy).then_inc(bank_of(("h2T", t2)), 1)
                copied(act, l, "rT")
                act.activation(r_s, r_z, ACT.Exp, scale=-1.0).then_inc(rexp_ready.sem, 1)

                def tokens(base, e, b):
                    act.wait_ge(hsT_full, base + e + 1 + CREDIT)
                    act.wait_ge(up_full, base + e - 1 + CREDIT)
                    act.activation(hsT[b][:, 4:8, :], ps[:, 512:1024].rearrange("p (a b) -> p a b", a=4), ACT.Copy)\
                        .then_inc(hsT_ready, 1)

                def hidden_back(base, e, b):
                    act.wait_ge(hidT_full, base + e + 1)
                    act.wait_ge(dn_full, base + e + CREDIT)
                    act.activation(hidT, ps[:, (2 + b) * BANK:(2 + b) * BANK + FF].rearrange("p (a b) -> p a b", a=2),
                                   ACT.Copy).then_inc(hidT_ready, 1)

                def hidden(base, e, b):
                    act.wait_ge(up_full, base + e + 1 + CREDIT)
                    act.wait_ge(hid_ready, base + e)
                    act.activation(ff_t[:, b, :], ps[:, (2 + b) * BANK:(2 + b) * BANK + FF], ACT.Exp, scale=-1.0)\
                        .then_inc(e_ready, 1)

                def output(base, e, b):
                    act.wait_ge(dn_full, base + e + 1 + CREDIT)
                    act.wait_ge(ys_out[b], base * 8 + (e - b) * 8)
                    lo = (4 + 2 * b) * BANK
                    act.activation(ys[:, b, 512:1024], ps[:, lo + 512:lo + 1024], ACT.Copy).then_inc(ys_high, 1)

                def rounds():
                    act.wait_ge(routed.sem, routed.at(l, 1))
                    act.sem_inc(passed, 1)
                    n_rounds = act.value_load(rounds_i[0:1, 0:1], min_val=1, max_val=5)
                    with act.Fori(0, n_rounds):
                        base = act.snap(done, min_val=0, max_val=160)

                        def step(e, b):
                            hidden(base, e, b)
                            hidden_back(base, e - 1, 1 - b)
                            tokens(base, e + 1, 1 - b)
                            output(base, e - 1, 1 - b)

                        tokens(base, 0, 0)
                        hidden(base, 0, 0)
                        tokens(base, 1, 1)
                        with act.Fori(0, NE // 2 - 1) as i:
                            step(2 * i + 1, 1)
                            step(2 * i + 2, 0)
                        hidden(base, NE - 1, 1)
                        hidden_back(base, NE - 2, 0)
                        output(base, NE - 2, 0)
                        hidden_back(base, NE - 1, 1)
                        output(base, NE - 1, 1)
                        act.reg_add(done, done, NE)
                rounds()
                last = act.snap(done, min_val=16, max_val=160)
                act.wait_ge(ys_out[0], last * 8)
                act.wait_ge(ys_out[1], last * 8)
                for t in range(TT):
                    act.dma_start(y_1st[:, t, :], y_by[t, 0]).then_inc(yg_in[t].sem, 16)
                    act.dma_start(y_2nd[:, t, :], y_by[t, 1]).then_inc(yg_in[t].sem, 16)
                for t in range(TT + 1):
                    if t < TT:
                        act.wait_ge(yg_in[t].sem, yg_in[t].at(l, 32))
                        act.activation(y_1st[:, t, :], y_1st[:, t, :], ACT.Copy, scale=gates[:, 0, t:t + 1])\
                            .then_inc(y_first.sem, 1)
                    if t:
                        act.wait_ge(x_done.sem, x_done.at(l, t))
                        mean_square(squares.at(l + 1, t - 1), t - 1)
            for t in range(TT):
                act.wait_ge(y_final, t + 1)
                act.dma_start(O["y"][t * P:(t + 1) * P, :], h2[:, t, :]).then_inc(y_out, 16)

        @block.vector
        def _(dve):
            V = dve.tensor_tensor
            dve.wait_ge(cond_exp, 1)
            dve.tensor_scalar(c_exp, c_exp, 1.0, None, ALU.add).then_inc(cond_step, 1)
            dve.wait_ge(cond_step, 1)
            dve.reciprocal(c_exp, c_exp).then_inc(cond_step, 1)
            dve.wait_ge(cond_step, 2)
            V(c_raw, c_raw, c_exp, ALU.mult).then_inc(cond_step, 1)
            dve.wait_ge(cond_step, 3)
            dve.tensor_copy(cond.rearrange("p k (c n) -> p k c n", c=2),
                            c_raw.unsqueeze(3).broadcast_to((P, KD, 2, 16))).then_inc(cond_ready, 1)
            dve.wait_ge(const_in, 16 * 11)
            done = dve.alloc_register("experts_done_dve")
            dve.reg_mov(done, 0)
            links = [0]
            with dve.Fori(0, DEPTH) as l:

                def link(ins):
                    links[0] += 1
                    ins.then_inc(dve_chain.sem, 1)
                    dve.wait_ge(dve_chain.sem, dve_chain.at(l, links[0]))

                dve.wait_ge(ada_in.sem, ada_in.at(l, ada_in.per_layer))
                V(mods, filled(dve, l, "ada"), b_ada, ALU.add).then_inc(bank_of("ada"), 1)
                dve.wait_ge(x_in, 16 * (TT + 1))
                for t in range(TT):
                    dve.wait_ge(root_x.sem, root_x.at(l, t + 1))
                    dve.tensor_scalar(xn[:, t, :], x[:, t, :], rstd[:, 0, t:t + 1], None, ALU.mult).then_inc(xn_ready.sem, 1)
                out = filled(dve, l, "modT").rearrange("p (i q) -> p i q", i=4)
                for c in range(2):
                    for v in range(2):
                        src = out[:, :, 64 * v + 16 * c:64 * v + 16 * c + 33:32].rearrange("p i j -> p j i")
                        dst = (mod_s, mod_a)[v][:, c, :].rearrange("p (j i) -> p j i", j=2)
                        if v:
                            ins = dve.scalar_tensor_tensor(out=dst, in0=src, scalar=1.0,
                                                           in1=n1c.rearrange("p (j i) -> p j i", j=2),
                                                           op0=ALU.add, op1=ALU.mult)
                        else:
                            ins = dve.tensor_copy(dst, src)
                ins.then_inc(bank_of("modT"), 1)
                copied(dve, l, "modT")
                for k in range(KD):
                    out = filled(dve, l, ("h1T", k))
                    dve.tensor_scalar(hT[:, k, 0:N_LAT], out[:, 0:N_LAT], mod_a[:, 0, k:k + 1], mod_s[:, 0, k:k + 1],
                                      ALU.mult, ALU.add).then_inc(bank_of(("h1T", k)), 1)
                dve.wait_ge(bias_ready.sem, bias_ready.at(l, 1))
                for zero in (z_lat[:, 0:1], z_lat[:, 527:528], z_ctx[:, 0:1]):
                    dve.memset(zero, 0.0)
                link(dve.memset(z_ctx[:, 129:130], 0.0))
                for c in range(2):
                    out = filled(dve, l, ("pT", 3 * c + 1))
                    copied(dve, l, ("pT", 3 * c))
                    V(z_lat[:, 8:520], out[:, 0:N_LAT], c_sb[:, 0:N_LAT], ALU.mult)
                    V(z_ctx[:, 1:129], out[:, N_LAT:N_TOK], c_sb[:, N_LAT:N_TOK], ALU.mult).then_inc(bank_of(("pT", 3 * c + 1)), 1)
                    copied(dve, l, ("pT", 3 * c + 1))
                    dve.tensor_copy(z_lat[:, 1:8], z_lat[:, 512:519])
                    link(dve.tensor_copy(z_lat[:, 520:527], z_lat[:, 9:16]))
                    w = [convw[:, c, i:i + 1] for i in range(3)]
                    parts = [(cv[:, 0:N_LAT], z_lat, 8, N_LAT), (cv[:, N_LAT:N_TOK], z_ctx, 1, N_CTX)]
                    for i, n in enumerate((1, 0, 2)):
                        for dst, z, s, m in parts:
                            if i == 0:
                                ins = dve.tensor_scalar(dst, z[:, s:s + m], w[1], None, ALU.mult)
                            else:
                                ins = dve.scalar_tensor_tensor(out=dst, in0=z[:, n * s:n * s + m], scalar=w[n], in1=dst,
                                                               op0=ALU.mult, op1=ALU.add)
                        link(ins)
                    out = filled(dve, l, ("pT", 3 * c + 2))
                    V(yT[:, c, :], out[:, 0:N_TOK], cv, ALU.mult).then_inc(bank_of(("pT", 3 * c + 2)), 1)
                dve.wait_ge(q_zeroed.sem, q_zeroed.at(l, 1))
                for p in range(2):
                    out = filled(dve, l, ("pT", 8 + p))
                    dve.tensor_copy(k_n[:, p, 0:N_LAT], out[:, 0:N_LAT])
                    dve.tensor_copy(k_n[:, p, 640:768], out[:, N_LAT:N_TOK]).then_inc(bank_of(("pT", 8 + p)), 1)
                dve.wait_ge(small_in.sem, small_in.at(l, small_in.per_layer))
                for t in range(TT):
                    out = filled(dve, l, ("pN", t))
                    dve.tensor_copy(v_n[:, t, :], out[:, 0:256])
                    dve.tensor_copy(ckv_n[:, t, :], out[:, 256:384]).then_inc(ckv_raw.sem, 1)
                    dve.tensor_copy(kr[:, t, :], out[:, 384:416]).then_inc(bank_of(("pN", t)), 1)
                for t in range(TT):
                    dve.wait_ge(root_kv.sem, root_kv.at(l, t + 1))
                    dve.scalar_tensor_tensor(out=ckv_n[:, t, :], in0=ckv_n[:, t, :], scalar=rstd[:, 2, t:t + 1], in1=gkv,
                                             op0=ALU.mult, op1=ALU.mult).then_inc(ckv_ready.sem, 1)

                def rotate(v, cos, sin, shape):
                    n = int(np.prod(shape))
                    tm = [tmp4[:, i, 0:n].rearrange("p (a b f) -> p a b f", a=shape[0], b=shape[1]) for i in range(4)]
                    x1, x2 = v[:, :, :, 0, :], v[:, :, :, 1, :]
                    V(tm[0], x1, cos, ALU.mult)
                    V(tm[1], x2, sin, ALU.mult)
                    V(tm[2], x1, sin, ALU.mult)
                    link(V(tm[3], x2, cos, ALU.mult))
                    V(x1, tm[0], tm[1], ALU.subtract)
                    return V(x2, tm[3], tm[2], ALU.add)

                copied(dve, l, ("pN", TT - 1))
                r4 = rope.rearrange("p c t (a f) -> p c t a f", a=2)
                rotate(kr[:, 0:TL, :].rearrange("p t (a h f) -> p t a h f", a=2, h=2), r4[:, 0], r4[:, 1], (TL, 2, 8))\
                    .then_inc(kr_ready.sem, 1)
                for ch in range(2):
                    out = filled(dve, l, ("fnA", ch, 0))
                    dve.tensor_copy(dftT[:, 0, ch, :], out[:, 0:N_TOK]).then_inc(bank_of(("fnA", ch, 0)), 1)
                out = filled(dve, l, "ckT")
                dve.tensor_copy(ckvT[:, 0:N_LAT], out[:, 0:N_LAT])
                dve.tensor_copy(ckvT[:, 640:768], out[:, N_LAT:N_TOK]).then_inc(bank_of("ckT"), 1)
                out = filled(dve, l, "krT")
                for h in range(HEADS):
                    ins = dve.tensor_copy(k_m[64:96, h, 640:768], out[0:ROPE, N_LAT:N_TOK])
                ins.then_inc(bank_of("krT"), 1)
                for o in range(2):
                    out = filled(dve, l, ("fnY", o))
                    dve.tensor_copy(yT[:, 6 + o, :], out[:, 0:N_TOK]).then_inc(bank_of(("fnY", o)), 1)
                for t in range(TT):
                    copied(dve, l, ("qup", t))
                    q = q_up[:, t % 2, :].rearrange("p (h n) -> p h n", h=HEADS)[:, :, HD:QK]
                    if t < TL:
                        shape = (P, HEADS, 2, 8)
                        rotate(q.rearrange("p h (a x f) -> p h a x f", a=2, x=2), r4[:, 0, t].unsqueeze(1).broadcast_to(shape),
                               r4[:, 1, t].unsqueeze(1).broadcast_to(shape), (HEADS, 2, 8)).then_inc(q_up_ready.sem, 1)
                    else:
                        dve.tensor_copy(tmp4[:, 0, 0:1], tmp4[:, 1, 0:1]).then_inc(q_up_ready.sem, 1)
                    out = filled(dve, l, ("qT", t))
                    dve.tensor_copy(q_m[0:QK, :, t * P:(t + 1) * P],
                                    out[0:QK, 0:512].rearrange("p (h n) -> p h n", h=HEADS)).then_inc(bank_of(("qT", t)), 1)
                for step in range(len(UNITS) + LEAD + 1):
                    if step < len(UNITS):
                        u = step
                        kind, h, t = UNITS[u]
                        wd = WIDTH[kind]
                        out = filled(dve, l, ("S", u))
                        col = slice(u % 4, u % 4 + 1)
                        src, factor = out[:, 0:wd], -(QK if kind[0] == "m" else HD) ** -0.5
                        if kind == "na":
                            dve.scalar_tensor_tensor(out=probs[:, u % 4, 0:256], in0=out[:, 0:256], scalar=HD ** -0.5,
                                                     in1=bias[:, h, BIAS_KIND[t], :], op0=ALU.mult, op1=ALU.add)
                            dve.tensor_scalar(probs[:, u % 4, 256:384], out[:, 256:384], HD ** -0.5, None, ALU.mult)\
                                .then_inc(bank_of(("S", u)), 1)
                            copied(dve, l, ("S", u))
                            src, factor = probs[:, u % 4, 0:wd], -1.0
                        link(dve.tensor_reduce(rowmax[:, col], src, AX.X, ALU.max))
                        dve.tensor_scalar(negmax[:, col], rowmax[:, col], factor, None, ALU.mult).then_inc(max_ready.sem, 1)
                    if 0 < step <= len(UNITS):
                        u = step - 1
                        kind = UNITS[u][0]
                        col = slice(u % 4, u % 4 + 1)
                        if kind == "na":
                            dve.wait_ge(exp_ready.sem, exp_ready.at(l, u + 1))
                        else:
                            copied(dve, l, ("S", u))
                        if kind == "ml":
                            link(dve.reciprocal(rowinv[:, col], rowsum[:, col]))
                            dve.tensor_scalar(probs[:, u % 4, :], probs[:, u % 4, :], rowinv[:, col], None, ALU.mult)\
                                .then_inc(probs_divided.sem, 1)
                        else:
                            dve.reciprocal(rowinv[:, col], rowsum[:, col]).then_inc(inv_ready.sem, 1)
                    if step > LEAD and output_after(step - LEAD - 1):
                        key = output_after(step - LEAD - 1)
                        kind, p, t = key
                        out = filled(dve, l, key)
                        k = p + (2 if kind[0] == "n" else 4)
                        dst = yT[:, k, 0:N_LAT] if kind == "mlO" else yT[:, k, t * P:(t + 1) * P]
                        dve.tensor_copy(dst, out[:, 0:N_LAT if kind == "mlO" else P]).then_inc(bank_of(key), 1)
                    if step in MOD_STEPS:
                        i = MOD_STEPS.index(step)
                        if i == 0:
                            dve.wait_ge(ada2_in.sem, ada2_in.at(l, 32))
                        elif i % 4:
                            copied(dve, l, ("mod2", i - 1))
                        V(mods2[:, i // 4, :], filled(dve, l, ("mod2", i)), mods2[:, i // 4, :] if i % 4 else b_ada2[:, i // 4, :],
                          ALU.add).then_inc(bank_of(("mod2", i)), 1)
                        if i == 7:
                            copied(dve, l, ("mod2", i))
                            dve.scalar_tensor_tensor(out=mods2[0:64, 1, :], in0=mods2[0:64, 1, :], scalar=1.0,
                                                     in1=n2q[0:64, :], op0=ALU.add, op1=ALU.mult).then_inc(mods_scaled.sem, 1)
                dve.wait_ge(gate1_in.sem, gate1_in.at(l, 32))
                dve.wait_ge(mod2_in.sem, mod2_in.at(l, 64))
                for t in range(TT):
                    out = filled(dve, l, ("out", t))
                    V(hs[:, t % 2, :], out[:, 0:D], rows[:, 0, t // TL, :], ALU.mult).then_inc(bank_of(("out", t)), 1)
                    copied(dve, l, ("out", t))
                    V(x[:, t, :], x[:, t, :], hs[:, t % 2, :], ALU.add).then_inc(x_mixed.sem, 1)
                    dve.wait_ge(root_mixed.sem, root_mixed.at(l, t + 1))
                    dve.scalar_tensor_tensor(out=h2[:, t, :], in0=x[:, t, :], scalar=rstd[:, 3, t:t + 1],
                                             in1=rows[:, 1, t // TL, :], op0=ALU.mult, op1=ALU.mult)\
                        .then_inc(h2_scaled.sem, 1)
                    for t2 in {0: (), TL: (TL - 1, TL)}.get(t, (t - 1,)):
                        out = filled(dve, l, ("h2T", t2))
                        dve.tensor_copy(h2T[:, 0:4, t2 * P:(t2 + 1) * P], out[:, 0:512].rearrange("p (k n) -> p k n", k=4))\
                            .then_inc(bank_of(("h2T", t2)), 1)
                out = filled(dve, l, "rl")
                dve.tensor_copy(r_log, out[:, 0:N_TOK]).then_inc(bank_of("rl"), 1)
                out = filled(dve, l, "rT")[:, 0:N_TOK].rearrange("p (t j e) -> p t e j", t=TT, j=4)
                dve.tensor_reduce(r_z, out[:, :, 0:NE, :], AX.X, ALU.add).then_inc(bank_of("rT"), 1)
                dve.wait_ge(rexp_ready.sem, rexp_ready.at(l, 1))
                link(dve.tensor_scalar(r_s, r_s, 1.0, None, ALU.add))
                link(dve.reciprocal(r_s, r_s))
                link(V(r_sb, r_s, b_r.unsqueeze(1).broadcast_to((P, TT, NE)), ALU.add))
                grp = r_sb.rearrange("p t (g e) -> p (t g) e", g=4)
                V(r_pair[:, :, 0:3], grp[:, :, 0:3], grp[:, :, 1:4], ALU.add)
                V(r_pair[:, :, 3:5], grp[:, :, 0:2], grp[:, :, 2:4], ALU.add)
                link(V(r_pair[:, :, 5:6], grp[:, :, 0:1], grp[:, :, 3:4], ALU.add))

                def first_of_max(dst, val, count, n, tmp, mx):
                    bc = (P, TT, n)
                    link(dve.tensor_reduce(mx, val, AX.X, ALU.max))
                    link(V(tmp, val, mx.unsqueeze(2).broadcast_to(bc), ALU.is_equal))
                    link(V(tmp, tmp, count.unsqueeze(1).broadcast_to(bc), ALU.mult))
                    link(dve.tensor_reduce(mx, tmp, AX.X, ALU.max))
                    link(V(dst, tmp, mx.unsqueeze(2).broadcast_to(bc), ALU.is_equal))

                link(dve.tensor_reduce(r_g.rearrange("p t g -> p (t g)"), r_pair, AX.X, ALU.max))
                first_of_max(r_first, r_g, count4, 4, r_t[:, :, 0:4], r_gm)
                flag = r_first.rearrange("p t g -> p (t g)").unsqueeze(2).broadcast_to((P, 4 * TT, 4))
                V(r_m.rearrange("p t (g e) -> p (t g) e", g=4), grp, flag, ALU.mult)
                link(dve.tensor_scalar(r_t.rearrange("p t (g e) -> p (t g) e", g=4), flag, -MASKED, MASKED, ALU.mult, ALU.add))
                link(V(r_m, r_m, r_t, ALU.add))
                for a in range(2):
                    first_of_max(r_sel[:, a], r_m, count16, NE, r_t, r_gm)
                    if a == 0:
                        link(dve.scalar_tensor_tensor(out=r_m, in0=r_sel[:, 0], scalar=10 * MASKED, in1=r_m,
                                                      op0=ALU.mult, op1=ALU.add))
                V(r_mask, r_sel[:, 0], r_sel[:, 1], ALU.add).then_inc(mask_ready.sem, 1)
                for a in range(2):
                    link(V(r_t, r_sel[:, a], r_s, ALU.mult))
                    link(dve.tensor_reduce(r_w[:, a], r_t, AX.X, ALU.add))
                link(V(r_gm, r_w[:, 0], r_w[:, 1], ALU.add))
                link(dve.reciprocal(r_gm, r_gm))
                V(gates, r_w, r_gm.unsqueeze(1).broadcast_to((P, 2, TT)), ALU.mult)
                out = filled(dve, l, "rank")
                link(dve.memset(r_cum[:, 0, :], 0.0))
                for t in range(TT):
                    link(V(r_cum[:, t + 1, :], out[:, 128 + t * NE:128 + (t + 1) * NE], r_cum[:, t, :], ALU.add))
                V(r_rank, out[:, 0:80].rearrange("p (t e) -> p t e", t=TT), r_cum[:, 0:TT, :], ALU.add).then_inc(bank_of("rank"), 1)
                copied(dve, l, "rank")
                link(dve.scalar_tensor_tensor(out=r_rank, in0=r_rank, scalar=float(NE),
                                              in1=iota16.unsqueeze(1).broadcast_to((P, TT, NE)), op0=ALU.mult, op1=ALU.add))
                for a in range(2):
                    link(V(r_t, r_sel[:, a], r_rank, ALU.mult))
                    link(dve.tensor_reduce(r_pos[:, a], r_t, AX.X, ALU.add))
                dve.tensor_copy(pos_i[:, :], r_pos.rearrange("p a t -> p (a t)"))
                link(dve.tensor_reduce(r_n[:, 0:1], r_cum[:, TT, :], AX.X, ALU.max))
                link(dve.tensor_scalar(r_n[:, 1:5], limits, r_n[:, 0:1], None, ALU.is_lt))
                link(dve.tensor_reduce(r_n[:, 5:6], r_n[:, 1:5], AX.X, ALU.add))
                dve.tensor_scalar(rounds_i[:, 0:1], r_n[:, 5:6], 1.0, None, ALU.add).then_inc(routed.sem, 1)

                def tokens(base, e, b):
                    dve.wait_ge(hsT_full, base + e + 1 + CREDIT)
                    dve.wait_ge(up_full, base + e - 1 + CREDIT)
                    dve.tensor_copy(hsT[b][:, 0:4, :], ps[:, 0:512].rearrange("p (a b) -> p a b", a=4)).then_inc(hsT_ready, 1)

                def hidden(base, e, b):
                    dve.wait_ge(e_ready, base + e + 1)
                    dve.wait_ge(up_full, base + e + 1 + CREDIT)
                    lo = (2 + b) * BANK
                    f = ff_t[:, b, :]
                    dve.tensor_scalar(f, f, 1.0, None, ALU.add).then_inc(silu_chain, 1)
                    dve.wait_ge(silu_chain, (base + e) * 3 + 1)
                    dve.reciprocal(f, f).then_inc(silu_chain, 1)
                    dve.wait_ge(silu_chain, (base + e) * 3 + 2)
                    V(f, ps[:, lo:lo + FF], f, ALU.mult).then_inc(silu_chain, 1)
                    dve.wait_ge(silu_chain, (base + e) * 3 + 3)
                    V(hid[:, b, :], ps[:, lo + FF:lo + 2 * FF], f, ALU.mult).then_inc(hid_ready, 1)

                def output(base, e, b):
                    dve.wait_ge(dn_full, base + e + 1 + CREDIT)
                    dve.wait_ge(ys_out[b], base * 8 + (e - b) * 8)
                    lo = (4 + 2 * b) * BANK
                    dve.tensor_copy(ys[:, b, 0:512], ps[:, lo:lo + 512]).then_inc(ys_low, 1)

                def rounds():
                    n_rounds = dve.value_load(rounds_i[0:1, 0:1], min_val=1, max_val=5)
                    with dve.Fori(0, n_rounds):
                        base = dve.snap(done, min_val=0, max_val=160)

                        def step(e, b):
                            tokens(base, e + 1, 1 - b)
                            hidden(base, e, b)
                            output(base, e - 1, 1 - b)

                        tokens(base, 0, 0)
                        tokens(base, 1, 1)
                        hidden(base, 0, 0)
                        with dve.Fori(0, NE // 2 - 1) as i:
                            step(2 * i + 1, 1)
                            step(2 * i + 2, 0)
                        hidden(base, NE - 1, 1)
                        output(base, NE - 2, 0)
                        output(base, NE - 1, 1)
                        dve.reg_add(done, done, NE)
                dve.wait_ge(routed.sem, routed.at(l, 1))
                dve.sem_inc(passed, 1)
                rounds()
                dve.wait_ge(gate2_in.sem, gate2_in.at(l, 32))
                for t in range(TT):
                    y_t = y_2nd[:, t, :]
                    dve.wait_ge(yg_in[t].sem, yg_in[t].at(l, 32))
                    dve.wait_ge(y_first.sem, y_first.at(l, t + 1))
                    link(dve.scalar_tensor_tensor(out=y_t, in0=y_t, scalar=gates[:, 1, t:t + 1],
                                                  in1=y_1st[:, t, :], op0=ALU.mult, op1=ALU.add))
                    link(V(y_t, y_t, rows[:, 0, t // TL, :], ALU.mult))
                    V(x[:, t, :], x[:, t, :], y_t, ALU.add).then_inc(x_done.sem, 1)
            assert links[0] == DVE_CHAIN, links[0]
            assert copies == plan.copies, {k: (copies.get(k), n) for k, n in plan.copies.items() if copies.get(k) != n}
            dve.wait_ge(normf_in, 16)
            for t in range(TT):
                dve.wait_ge(root_x.sem, root_x.at(DEPTH, t + 1))
                dve.scalar_tensor_tensor(out=h2[:, t, :], in0=x[:, t, :], scalar=rstd[:, 0, t:t + 1], in1=normf_row,
                                         op0=ALU.mult, op1=ALU.mult).then_inc(y_final, 1)


def grid_order():
    return np.arange(N_LAT).reshape(GRID_H, GRID_W).T.ravel()


def shape_constants():
    order = grid_order()
    c = {}
    c["c_ident"] = np.eye(P, dtype=np.float32)
    c["c_before"] = np.triu(np.ones((P, P), np.float32), 1)
    c["c_ones"] = np.ones((P, P), np.float32)
    ang = 2 * np.pi * (np.outer(np.arange(HD), np.arange(HD)) % HD) / HD
    chan = np.zeros((P, 2, P))
    for g in range(2):
        s = slice(g * HD, (g + 1) * HD)
        chan[s, 0, s], chan[s, 1, s] = np.cos(ang), -np.sin(ang)
    c["c_chan"] = chan.astype(np.float32)

    def dft(places, n):
        a = 2 * np.pi * (np.outer(places, places) % n) / n
        return np.stack([np.cos(a), np.sin(a)]) / np.sqrt(n * HD)

    lat = dft(order, N_LAT).reshape(2, TL, P, N_LAT).transpose(2, 0, 1, 3)
    c["c_dft"] = np.ascontiguousarray(lat.reshape(P, -1)).astype(np.float32)
    ctx = dft(np.arange(N_CTX), N_CTX).transpose(1, 0, 2)
    c["c_dft_ctx"] = np.ascontiguousarray(ctx.reshape(P, -1)).astype(np.float32)
    pos = np.stack([order // GRID_W, order % GRID_W], -1).astype(np.float32)
    nf = ROPE // 4
    freqs = np.float32(10000.0) ** (-np.arange(nf, dtype=np.float32) / nf)
    ang = (pos[:, :, None] * freqs).astype(np.float32)
    rope = np.stack([np.cos(ang), np.sin(ang)]).reshape(2, TL, P, 2 * nf).transpose(2, 0, 1, 3)
    c["c_rope"] = np.ascontiguousarray(rope).astype(np.float32)
    c["c_iota"] = np.tile(np.arange(NE, dtype=np.float32), (P, 1))
    c["c_count"] = np.tile(np.arange(NE, 0, -1, dtype=np.float32), (P, 1))
    c["c_limits"] = np.tile(np.arange(1, 5, dtype=np.float32) * P, (P, 1))
    token = np.arange(P)[:, None, None] + P * np.arange(TT)[None, None] + np.zeros((1, 2, 1), np.int64)
    c["c_tok"] = np.stack([token, 2 * token + np.arange(2)[None, :, None]], -1).astype(np.int32)
    masks = np.zeros((P, 3, 256), np.float32)
    for kind, t in enumerate((0, 1, 3)):
        q = (np.arange(P) // GRID_H + 16 * t)[:, None]
        k = (np.arange(256) // GRID_H + WIN[t] // GRID_H)[None]
        start = np.clip(q - NK // 2, 0, GRID_W - NK)
        masks[:, kind] = np.where((k >= start) & (k < start + NK), 0.0, MASKED)
    c["c_masks"] = masks
    return c


def laid_out(inputs):
    a = {k: np.asarray(v) for k, v in inputs.items()}
    order = grid_order()
    o = {}
    o["x_all"] = np.concatenate([a["x_sample"][0][order], a["x_prompt"][0]])
    o["c_cols"] = np.stack([a["c"][0].reshape(KD, P).T, a["c_ctx"].reshape(KD, P).T], axis=2)
    o["w_ada"] = a["w_ada"]
    o["b_ada_q"] = a["b_ada"].reshape(DEPTH, 3, 4, 512).transpose(0, 2, 1, 3).reshape(DEPTH, 4, 1536)
    o["norm1_c"] = a["norm1"].reshape(DEPTH, KD, P).transpose(0, 2, 1)
    o["norm2"] = a["norm2"]
    w = a["w_in"]
    at = {"b": 0, "c": 256, "u": 512, "q": 768, "k": 1024}
    tiles = [w[:, :, at[n[0]] + P * int(n[1]):at[n[0]] + P * (int(n[1]) + 1)] for n in PROJ_T]
    wt = np.stack(tiles, 1).reshape(DEPTH, 5, 2, KD, P, P).transpose(0, 1, 4, 2, 3, 5)
    o["w_t"] = wt.reshape(DEPTH, 5, P, 2 * KD * P)
    wn = np.concatenate([w[:, :, 1280:1536], w[:, :, 1792:1952], w[:, :, 1536:1792], w[:, :, 1952:2208]], 2)
    o["w_n"] = wn.reshape(DEPTH, 4, 2, P, 928).transpose(0, 1, 3, 2, 4).reshape(DEPTH, 4, P, 2 * 928)
    o["conv_c"] = a["conv_w"].reshape(DEPTH, 3, 2, P).transpose(0, 3, 2, 1)
    o["rpb_t"] = a["na_rpb"].transpose(0, 1, 3, 2)
    o["gq_c"] = a["mla_gq"].reshape(DEPTH, 2, P).transpose(0, 2, 1)
    for n in ("mla_gkv", "w_fn", "mla_wq_up", "w_out", "w_router", "b_router", "w2"):
        o[n] = a[n]
    o["mla_wkv_up"] = a["mla_wkv_up"].reshape(DEPTH, P, HEADS, 2, HD).transpose(0, 1, 3, 2, 4).reshape(DEPTH, P, 512)
    o["norm_f"] = a["norm_f"].reshape(1, D)
    o["nk_t"] = a["cache_na_k"][0].reshape(DEPTH, 2, 2, P, HD).transpose(0, 2, 4, 1, 3).reshape(DEPTH, P, 2, P)
    o["nv_t"] = a["cache_na_v"][0].transpose(0, 2, 1, 3).reshape(DEPTH, P, 256)
    o["ckv_t"] = a["cache_mla_ckv"][0].transpose(0, 2, 1)
    o["krope_t"] = a["cache_mla_krope"][0].transpose(0, 2, 1)
    w13 = np.concatenate([a["w1"].reshape(DEPTH, NE, KD, P, FF), a["w3"].reshape(DEPTH, NE, KD, P, FF)], 4)
    o["w_13"] = w13.transpose(0, 1, 3, 2, 4).reshape(DEPTH, NE, P, KD * 2 * FF)
    return {k: np.ascontiguousarray(v) for k, v in o.items()}


OUTS = {"y": (N_TOK, D), "nk": (DEPTH, P, 2, P), "nv": (DEPTH, P, 256), "ckv": (DEPTH, P, P), "kr": (DEPTH, P, ROPE)}


def kernel(**inputs):
    import concourse.bacc as bacc
    from concourse.bass_utils import run_bass_kernel_spmd

    nc = bacc.Bacc("TRN2", target_bir_lowering=False, num_devices=1)
    arrays, A, O = {}, {}, {}
    for name, a in {**laid_out(inputs), **shape_constants()}.items():
        arrays[f"in_{name}"] = a
        A[name] = nc.dram_tensor(f"in_{name}", a.shape, mybir.dt.from_np(a.dtype), kind="ExternalInput").ap()
    for name, shape in OUTS.items():
        O[name] = nc.dram_tensor(f"out_{name}", shape, F32, kind="ExternalOutput").ap()
    mixer_kernel(nc, A, O)
    r = run_bass_kernel_spmd(nc, [arrays], core_ids=[0]).results[0]
    y, nk, nv, ckv, kr = (np.asarray(r[f"out_{n}"]) for n in OUTS)
    y_sample = y[0:N_LAT].reshape(GRID_W, GRID_H, D).transpose(1, 0, 2).reshape(1, N_LAT, D)
    new_k = nk.reshape(DEPTH, 2, HD, 2, P).transpose(0, 3, 1, 4, 2).reshape(1, DEPTH, HEADS, P, HD)
    new_v = nv.reshape(DEPTH, P, HEADS, HD).transpose(0, 2, 1, 3).reshape(1, DEPTH, HEADS, P, HD)
    return (y[N_LAT:].reshape(1, N_CTX, D), y_sample, new_k, new_v,
            ckv.reshape(1, DEPTH, P, P), kr.reshape(1, DEPTH, P, ROPE))
```
